# Optimizing a Trainium2 kernel written in Bass

```python
import jax, jax.numpy as jnp
from jax import lax
import numpy as np

D_MODEL = 1024
BATCH = 1
SEQ = 256
DEPTH = 2

HEAD_DIM = 64
ROPE_THETA = 10000.0
NORM_EPS = 1e-6
GMLP_GROUPS = 4
GMLP_WIDTH = GMLP_GROUPS * HEAD_DIM
GMLP_CHUNK = 128
DIL_CONFIGS = ((128, 1), (512, 4), (2048, 16))
DIL_HEADS_PER_GROUP = 4
DIL_HEADS = DIL_HEADS_PER_GROUP * len(DIL_CONFIGS)
DIL_WIDTH = DIL_HEADS * HEAD_DIM
DIL_OUT_WIDTH = DIL_HEADS_PER_GROUP * HEAD_DIM
EVEN_IN = 2 * GMLP_WIDTH + 3 * DIL_WIDTH
EVEN_OUT = GMLP_WIDTH + DIL_OUT_WIDTH
MOBA_HEADS = 12
MOBA_WIDTH = MOBA_HEADS * HEAD_DIM
MOBA_BLOCK = 256
MOBA_TOPK = 3
MOBA_Q_CHUNK = 16
CONV_WIDTH = 256
CONV_TAPS = 3
ODD_IN = 3 * MOBA_WIDTH + 3 * CONV_WIDTH
ODD_OUT = MOBA_WIDTH + CONV_WIDTH
D_FF = 2816
N_EXPERTS = 8
TOP_K = 2
D_FF_EXPERT = 3584
N_EVEN = (DEPTH + 1) // 2
N_ODD = DEPTH // 2

kernel_name = "hybrid_gmlp_dilated_moba_shortconv_moe"

def rms_norm(x, g):
    xf = x.astype(jnp.float32)
    y = xf * lax.rsqrt(jnp.mean(xf * xf, axis=-1, keepdims=True) + NORM_EPS)
    return (y * g.astype(jnp.float32)).astype(x.dtype)

def rope_tables(seq):
    inv = 1.0 / (ROPE_THETA ** (jnp.arange(0, HEAD_DIM, 2, dtype=jnp.float32) / HEAD_DIM))
    ang = jnp.arange(seq, dtype=jnp.float32)[:, None] * inv[None, :]
    ang = jnp.concatenate([ang, ang], axis=-1)
    return jnp.cos(ang)[:, None, :], jnp.sin(ang)[:, None, :]

def apply_rope(x, cos, sin):
    xf = x.astype(jnp.float32)
    half = HEAD_DIM // 2
    rot = jnp.concatenate([-xf[..., half:], xf[..., :half]], axis=-1)
    return (xf * cos + rot * sin).astype(x.dtype)

def prep_qk(q, k, gq, gk, cos, sin):
    return apply_rope(rms_norm(q, gq), cos, sin), apply_rope(rms_norm(k, gk), cos, sin)

def swiglu(h, wg, wu, wd):
    return (jax.nn.silu(h @ wg) * (h @ wu)) @ wd

def gmlp_spatial_gating(z, v_gain, ws, bs):
    b, s, _ = z.shape
    z = jax.nn.gelu(z)
    u, v = z[..., :GMLP_WIDTH], z[..., GMLP_WIDTH:]
    v = rms_norm(v.reshape(b, s, GMLP_GROUPS, HEAD_DIM), v_gain.reshape(GMLP_GROUPS, HEAD_DIM))
    v = v.reshape(b, s // GMLP_CHUNK, GMLP_CHUNK, GMLP_GROUPS, HEAD_DIM)
    causal = jnp.tril(jnp.ones((GMLP_CHUNK, GMLP_CHUNK), dtype=bool))
    w = jnp.where(causal[None], ws, jnp.zeros_like(ws))
    y = jnp.einsum('gij,bcjgd->bcigd', w, v) + jnp.swapaxes(bs, 0, 1)[:, :, None]
    return u * y.reshape(b, s, GMLP_WIDTH)

def banded_causal_attention(q, k, v, band):
    n, L, h, dh = q.shape
    nb = -(-L // band)
    pad = nb * band - L

    def blocks(t):
        return jnp.pad(t, ((0, 0), (0, pad), (0, 0), (0, 0))).reshape(n, nb, band, h, dh)

    def with_prev(t):
        prev = jnp.pad(t[:, :-1], ((0, 0), (1, 0), (0, 0), (0, 0), (0, 0)))
        return jnp.concatenate([prev, t], axis=2)

    qb, kw, vw = blocks(q), with_prev(blocks(k)), with_prev(blocks(v))
    sc = jnp.einsum('nbqhd,nbkhd->nbhqk', qb, kw, preferred_element_type=jnp.float32) * (HEAD_DIM ** -0.5)
    qi = jnp.arange(band)[:, None] + band
    kj = jnp.arange(2 * band)[None, :]
    dist = qi - kj
    blk = jnp.arange(nb)[:, None, None]
    mask = (dist >= 0) & (dist <= band) & (blk * band - band + kj >= 0)
    sc = jnp.where(mask[None, :, None], sc, -jnp.inf)
    m = jnp.max(sc, axis=-1, keepdims=True)
    p = jnp.exp(sc - m)
    l = jnp.sum(p, axis=-1, keepdims=True)
    o = jnp.einsum('nbhqk,nbkhd->nbhqd', p, vw.astype(jnp.float32)) / l
    lse = (m + jnp.log(l))[..., 0]
    o = o.transpose(0, 1, 3, 2, 4).reshape(n, nb * band, h, dh)[:, :L]
    lse = lse.transpose(0, 1, 3, 2).reshape(n, nb * band, h)[:, :L]
    return o, lse

def to_strided(t, dil):
    b, s, h, dh = t.shape
    return t.reshape(b, s // dil, dil, h, dh).transpose(0, 2, 1, 3, 4).reshape(b * dil, s // dil, h, dh)

def from_strided(t, b, dil):
    rest = t.shape[2:]
    L = t.shape[1]
    t = t.reshape((b, dil, L) + rest)
    t = jnp.moveaxis(t, 1, 2)
    return t.reshape((b, L * dil) + rest)

def dilated_attention(q, k, v):
    b = q.shape[0]
    outs, lses = [], []
    for g, (window, dil) in enumerate(DIL_CONFIGS):
        hs = slice(g * DIL_HEADS_PER_GROUP, (g + 1) * DIL_HEADS_PER_GROUP)
        o, lse = banded_causal_attention(to_strided(q[:, :, hs], dil), to_strided(k[:, :, hs], dil),
                                         to_strided(v[:, :, hs], dil), window // dil)
        outs.append(from_strided(o, b, dil))
        lses.append(from_strided(lse, b, dil))
    w = jax.nn.softmax(jnp.stack(lses, axis=0), axis=0)
    return jnp.sum(w[..., None] * jnp.stack(outs, axis=0), axis=0)

def moba_attention(q, k, v):
    b, s, h, dh = q.shape
    q, k, v = (t.transpose(0, 2, 1, 3) for t in (q, k, v))
    nblk = -(-s // MOBA_BLOCK)
    pad = nblk * MOBA_BLOCK - s
    kb = jnp.pad(k, ((0, 0), (0, 0), (0, pad), (0, 0))).reshape(b, h, nblk, MOBA_BLOCK, dh)
    vb = jnp.pad(v, ((0, 0), (0, 0), (0, pad), (0, 0))).reshape(b, h, nblk, MOBA_BLOCK, dh)
    kmean = jnp.mean(kb.astype(jnp.float32), axis=3)
    pos = jnp.arange(s)
    own = pos // MOBA_BLOCK
    gate = jnp.einsum('bhsd,bhnd->bhsn', q.astype(jnp.float32), kmean)
    fully_past = jnp.arange(nblk)[None, :] < own[:, None]
    gate = jnp.where(fully_past, gate, -jnp.inf)
    top_val, top_idx = lax.top_k(gate, min(MOBA_TOPK, nblk))
    idx = jnp.concatenate([top_idx.astype(jnp.int32),
                           jnp.broadcast_to(own[None, None, :, None], (b, h, s, 1)).astype(jnp.int32)], axis=-1)
    valid = jnp.concatenate([jnp.isfinite(top_val), jnp.ones((b, h, s, 1), dtype=bool)], axis=-1)
    nc = s // MOBA_Q_CHUNK

    def chunks(t):
        return jnp.moveaxis(t.reshape((b, h, nc, MOBA_Q_CHUNK) + t.shape[3:]), 2, 0)

    bi = jnp.arange(b)[:, None, None, None]
    hi = jnp.arange(h)[None, :, None, None]
    offs = jnp.arange(MOBA_BLOCK)

    def attend(args):
        qc, ic, vc, pc = args
        kg = kb[bi, hi, ic]
        vg = vb[bi, hi, ic]
        sc = jnp.einsum('bhqd,bhqjnd->bhqjn', qc, kg, preferred_element_type=jnp.float32) * (HEAD_DIM ** -0.5)
        kpos = ic[..., None] * MOBA_BLOCK + offs
        mask = vc[..., None] & (kpos <= pc[None, None, :, None, None])
        sc = jnp.where(mask, sc, -jnp.inf)
        shp = sc.shape
        p = jax.nn.softmax(sc.reshape(shp[:3] + (-1,)), axis=-1).reshape(shp)
        return jnp.einsum('bhqjn,bhqjnd->bhqd', p, vg.astype(jnp.float32))

    out = lax.map(attend, (chunks(q), chunks(idx), chunks(valid), pos.reshape(nc, MOBA_Q_CHUNK)))
    out = jnp.moveaxis(out, 0, 2).reshape(b, h, s, dh)
    return out.transpose(0, 2, 1, 3)

def short_conv_mixer(bg, cg, xz, w):
    z = cg * xz
    s = z.shape[1]
    zp = jnp.pad(z, ((0, 0), (CONV_TAPS - 1, 0), (0, 0)))
    y = sum(w[t] * zp[:, t:t + s] for t in range(CONV_TAPS))
    return bg * y

def moe_swiglu(h, router_w, wg, wu, wd):
    logits = jnp.einsum('bsd,de->bse', h, router_w, preferred_element_type=jnp.float32)
    top_val, top_idx = lax.top_k(logits, TOP_K)
    gates = jax.nn.softmax(top_val, axis=-1)
    gate = jnp.einsum('bske,bsk->bse', jax.nn.one_hot(top_idx, N_EXPERTS, dtype=jnp.float32), gates).astype(h.dtype)
    out = jnp.zeros_like(h)
    for e in range(N_EXPERTS):
        out = out + gate[..., e:e + 1] * swiglu(h, wg[e], wu[e], wd[e])
    return out

def setup_inputs(seed: int = 0) -> dict:
    key = jax.random.key(seed)
    ks = jax.random.split(key, 22)

    def nrm(k, shape, scale):
        return jax.random.normal(k, shape, jnp.float32) * scale

    def gain(k, shape):
        return 1.0 + 0.02 * jax.random.normal(k, shape, jnp.float32)

    ne, no = N_EVEN, N_ODD
    return {
        'x': nrm(ks[0], (BATCH, SEQ, D_MODEL), 1.0),
        'norm_mix': gain(ks[1], (DEPTH, D_MODEL)),
        'norm_ffn': gain(ks[2], (DEPTH, D_MODEL)),
        'w_in_ab': nrm(ks[3], (ne, D_MODEL, EVEN_IN), D_MODEL ** -0.5),
        'gmlp_v_gain': gain(ks[4], (ne, GMLP_WIDTH)),
        'gmlp_ws': nrm(ks[5], (ne, GMLP_GROUPS, GMLP_CHUNK, GMLP_CHUNK), GMLP_CHUNK ** -0.5),
        'gmlp_bs': 1.0 + 0.1 * jax.random.normal(ks[6], (ne, GMLP_GROUPS, GMLP_CHUNK), jnp.float32),
        'dil_q_gain': gain(ks[7], (ne, HEAD_DIM)),
        'dil_k_gain': gain(ks[8], (ne, HEAD_DIM)),
        'w_out_ab': nrm(ks[9], (ne, EVEN_OUT, D_MODEL), EVEN_OUT ** -0.5),
        'ffn_w_gate': nrm(ks[10], (ne, D_MODEL, D_FF), D_MODEL ** -0.5),
        'ffn_w_up': nrm(ks[11], (ne, D_MODEL, D_FF), D_MODEL ** -0.5),
        'ffn_w_down': nrm(ks[12], (ne, D_FF, D_MODEL), D_FF ** -0.5),
        'w_in_cd': nrm(ks[13], (no, D_MODEL, ODD_IN), D_MODEL ** -0.5),
        'moba_q_gain': gain(ks[14], (no, HEAD_DIM)),
        'moba_k_gain': gain(ks[15], (no, HEAD_DIM)),
        'conv_w': nrm(ks[16], (no, CONV_TAPS, CONV_WIDTH), CONV_TAPS ** -0.5),
        'w_out_cd': nrm(ks[17], (no, ODD_OUT, D_MODEL), ODD_OUT ** -0.5),
        'router_w': nrm(ks[18], (no, D_MODEL, N_EXPERTS), D_MODEL ** -0.5),
        'moe_w_gate': nrm(ks[19], (no, N_EXPERTS, D_MODEL, D_FF_EXPERT), D_MODEL ** -0.5),
        'moe_w_up': nrm(ks[20], (no, N_EXPERTS, D_MODEL, D_FF_EXPERT), D_MODEL ** -0.5),
        'moe_w_down': nrm(ks[21], (no, N_EXPERTS, D_FF_EXPERT, D_MODEL), D_FF_EXPERT ** -0.5),
    }

def reference(x, norm_mix, norm_ffn, w_in_ab, gmlp_v_gain, gmlp_ws, gmlp_bs, dil_q_gain, dil_k_gain,
              w_out_ab, ffn_w_gate, ffn_w_up, ffn_w_down, w_in_cd, moba_q_gain, moba_k_gain, conv_w,
              w_out_cd, router_w, moe_w_gate, moe_w_up, moe_w_down):
    b, s, _ = x.shape
    cos, sin = rope_tables(s)
    for layer in range(DEPTH):
        i = layer // 2
        h = rms_norm(x, norm_mix[layer])
        if layer % 2 == 0:
            p = h @ w_in_ab[i]
            o1 = 2 * GMLP_WIDTH
            o2 = o1 + DIL_WIDTH
            o3 = o2 + DIL_WIDTH
            a_out = gmlp_spatial_gating(p[..., :o1], gmlp_v_gain[i], gmlp_ws[i], gmlp_bs[i])
            q = p[..., o1:o2].reshape(b, s, DIL_HEADS, HEAD_DIM)
            k = p[..., o2:o3].reshape(b, s, DIL_HEADS, HEAD_DIM)
            v = p[..., o3:].reshape(b, s, DIL_HEADS, HEAD_DIM)
            q, k = prep_qk(q, k, dil_q_gain[i], dil_k_gain[i], cos, sin)
            b_out = dilated_attention(q, k, v).reshape(b, s, DIL_OUT_WIDTH).astype(h.dtype)
            x = x + jnp.concatenate([a_out, b_out], axis=-1) @ w_out_ab[i]
            x = x + swiglu(rms_norm(x, norm_ffn[layer]), ffn_w_gate[i], ffn_w_up[i], ffn_w_down[i])
        else:
            p = h @ w_in_cd[i]
            o1 = MOBA_WIDTH
            o2 = 2 * MOBA_WIDTH
            o3 = 3 * MOBA_WIDTH
            o4 = o3 + CONV_WIDTH
            o5 = o4 + CONV_WIDTH
            q = p[..., :o1].reshape(b, s, MOBA_HEADS, HEAD_DIM)
            k = p[..., o1:o2].reshape(b, s, MOBA_HEADS, HEAD_DIM)
            v = p[..., o2:o3].reshape(b, s, MOBA_HEADS, HEAD_DIM)
            q, k = prep_qk(q, k, moba_q_gain[i], moba_k_gain[i], cos, sin)
            c_out = moba_attention(q, k, v).reshape(b, s, MOBA_WIDTH).astype(h.dtype)
            d_out = short_conv_mixer(p[..., o3:o4], p[..., o4:o5], p[..., o5:], conv_w[i])
            x = x + jnp.concatenate([c_out, d_out], axis=-1) @ w_out_cd[i]
            x = x + moe_swiglu(rms_norm(x, norm_ffn[layer]), router_w[i], moe_w_gate[i], moe_w_up[i], moe_w_down[i])
    return x


_drawn_inputs = setup_inputs


def setup_inputs(seed=0):
    import zlib

    import numpy as np

    out = dict(_drawn_inputs(seed))
    spreads = {}
    factors = {'gmlp_v_gain': 3.596,
     'dil_q_gain': 3.278,
     'dil_k_gain': 4.932,
     'moba_q_gain': 8.0,
     'moba_k_gain': 8.0}
    for name, (base, spread) in spreads.items():
        noise = np.random.default_rng([zlib.crc32(name.encode()), seed]).standard_normal(out[name].shape)
        drawn = base * np.exp(spread * noise) if base else spread * noise
        out[name] = __import__('jax').numpy.asarray(drawn.astype(out[name].dtype))
    for name, factor in factors.items():
        out[name] = (out[name] * factor).astype(out[name].dtype)
    return out
```

```python
from contextlib import ExitStack

import numpy as np

import concourse.bass as bass
from concourse import mybir

F32 = mybir.dt.float32
F32R = mybir.dt.float32r
BF16 = mybir.dt.bfloat16
I32 = mybir.dt.int32
ACT = mybir.ActivationFunctionType
ALU = mybir.AluOpType
AX = mybir.AxisListType

P = 128
SEQ, D = 256, 1024
TT = SEQ // P
KD = D // P
HD = 64
HH = HD // 2
GW = 256
GG = 4
HEADS = 12
QW = HEADS * HD
CW = 256
FF = 2816
FE = 3584
NE = 8
EPS = 1e-6
QSCALE = HD ** -0.5
NEG = -1e30

RING = 7
TILE = 4096
UNIT = 1024
SPLITS = 4
SLAB = 512
SLABS = FE // SLAB
JOB_TILES = 3 * SLABS
JOB_UNITS = JOB_TILES * TILE // UNIT
JOBS_MAX = NE + 3
JCOLS = JOBS_MAX + 1

C_ID, C_IOTA, C_UP, C_ONE = 0, 128, 256, 384
C_COS, C_SIN, C_LT = 512, 640, 768
C_COLS = C_LT + 64
M_DIL0, M_DIL1, M_CAUSAL = 0, 384, 1152
M_COLS = M_CAUSAL + 256

R_MIX, R_FFN, R_BS, R_CONV = 0, 16, 32, 36
R_ROWS = R_CONV + 6
B_DQ, B_DK, B_MQ, B_MK, B_GV = 0, 64, 128, 192, 256


def constant_tables():
    c = np.zeros((P, C_COLS), np.float32)
    p = np.arange(P)
    c[:, C_ID:C_ID + P] = np.eye(P)
    c[:, C_IOTA:C_IOTA + P] = np.arange(P)[None, :]
    c[:, C_UP:C_UP + P] = p[:, None] < p[None, :]
    c[:, C_ONE:C_ONE + P] = 1.0
    inv = (1.0 / (np.float32(10000.0) ** (np.arange(0, HD, 2, dtype=np.float32) / HD))).astype(np.float32)
    ang = np.arange(SEQ, dtype=np.float32)[:, None] * inv[None, :]
    cos, sin = np.cos(ang).astype(np.float32), np.sin(ang).astype(np.float32)
    for t in range(TT):
        rows = slice(t * P, t * P + P)
        c[:, C_COS + t * HD:C_COS + (t + 1) * HD] = np.concatenate([cos[rows], cos[rows]], 1)
        c[:, C_SIN + t * HD:C_SIN + (t + 1) * HD] = np.concatenate([-sin[rows], sin[rows]], 1)
    e = np.arange(NE)
    c[:, C_LT:C_LT + 64] = (e[None, :] < e[:, None]).reshape(1, 64)

    m = np.zeros((P, M_COLS), np.float32)
    for t, base in ((0, M_DIL0), (1, M_DIL1)):
        keys = P * (t + 1)
        q = (t * P + p)[:, None]
        k = np.arange(keys)[None, :]
        for g, (window, dil) in enumerate(((128, 1), (512, 4), (2048, 16))):
            seen = (k <= q) & ((q - k) % dil == 0) & ((q - k) // dil <= window // dil)
            m[:, base + g * keys:base + (g + 1) * keys] = np.where(seen, 0.0, NEG)
    m[:, M_CAUSAL + P:M_CAUSAL + 2 * P] = np.where(p[None, :] <= p[:, None], 0.0, NEG)
    return c, m


def weight_stream(w_in_ab, w_out_ab, ffn_g, ffn_u, ffn_d, w_in_cd, w_out_cd):
    tiles, units = [], []

    def tile(w, row0, nrow, col0, ncol):
        tiles.append((w[row0:row0 + nrow * P, col0:col0 + ncol].rearrange("(k p) f -> p k f", p=P), nrow, ncol))
        return len(tiles) - 1

    def by_rows(t):
        _, nrow, ncol = tiles[t]
        n = UNIT // ncol
        return [(t, r, n, 0, ncol) for r in range(0, nrow, n)]

    def by_columns(t):
        _, nrow, ncol = tiles[t]
        return [(t, 0, nrow, c, P) for c in range(0, ncol, P)]

    first = {"in_ab": 0}
    for c in (2 * GW, 2 * GW + SLAB, 2 * GW + 2 * SLAB, 0, 2 * GW + 3 * SLAB, 2 * GW + 4 * SLAB):
        units += by_rows(tile(w_in_ab, 0, KD, c, min(SLAB, 2 * GW + 3 * QW - c)))
    first["out_ab"] = len(units)
    units += by_rows(tile(w_out_ab, 0, 4, 0, D))
    first["ffn"] = len(units)
    widths = [min(SLAB, FF - c) for c in range(0, FF, SLAB)]
    for s in range(len(widths) + 1):
        if s < len(widths):
            tg = tile(ffn_g, 0, KD, s * SLAB, widths[s])
            tu = tile(ffn_u, 0, KD, s * SLAB, widths[s])
            for g, u in zip(by_columns(tg), by_columns(tu)):
                units += [g, u]
        if s >= 1:
            units += by_rows(tile(ffn_d, (s - 1) * SLAB, widths[s - 1] // P, 0, D))
    first["in_cd"] = len(units)
    for c in range(0, 3 * QW, SLAB):
        units += by_rows(tile(w_in_cd, 0, KD, c, min(SLAB, 3 * QW - c)))
    first["conv"] = len(units)
    for c in (3 * QW + CW, 3 * QW + 2 * CW, 3 * QW):
        units += by_columns(tile(w_in_cd, 0, KD, c, CW))
    first["out_cd"] = len(units)
    for r in (0, 4):
        units += by_rows(tile(w_out_cd, r * P, 4, 0, D))
    first["moe"] = len(units)
    return tiles, units, first, widths


def decoder_trunk(nc, x, norm_mix, norm_ffn, w_in_ab, gmlp_v_gain, gmlp_ws, gmlp_bs, dil_q_gain, dil_k_gain,
                  w_out_ab, ffn_w_gate, ffn_w_up, ffn_w_down, w_in_cd, moba_q_gain, moba_k_gain, conv_w,
                  w_out_cd, router_w, moe_w_gate, moe_w_up, moe_w_down, const_f32, const_mask, out):
    tiles, units, first, widths = weight_stream(w_in_ab[0], w_out_ab[0], ffn_w_gate[0], ffn_w_up[0],
                                                ffn_w_down[0], w_in_cd[0], w_out_cd[0])
    U_MOE, T_MOE = len(units), len(tiles)
    assert U_MOE % SPLITS == 0 and JOB_UNITS % SPLITS == 0 and T_MOE % RING == 0 and JOB_TILES % RING == 0
    tile_last = {}
    for u, un in enumerate(units):
        tile_last[un[0]] = u

    with ExitStack() as ctx:
        base = (nc.sbuf_base + 31) // 32 * 32
        place = [base]

        def at(name, shape, dt, offset):
            return nc.alloc_sbuf_tensor_at(name, [P, *shape], dt, offset=offset)

        def keep(name, shape, dt=F32):
            size = int(np.prod(shape)) * (2 if dt == BF16 else 4)
            t = at(name, shape, dt, place[0])
            place[0] += (size + 31) // 32 * 32
            return t

        raw = keep("raw_ring", [RING, TILE])
        wh = keep("w_hi", [SPLITS, UNIT], F32R)
        wl = keep("w_lo", [SPLITS, UNIT], F32R)
        xres = keep("x_residual", [TT, D])
        cst = keep("const", [C_COLS])
        colpar = keep("col_params", [48])
        router = keep("router", [KD, NE])
        router_hi = keep("router_hi", [KD, NE], F32R)
        router_lo = keep("router_lo", [KD, NE], F32R)
        small = keep("small", [352])
        meta = keep("meta", [8], I32)
        xs_lo = at("x_scaled_lo", [TT, D], F32R, place[0])
        msk = keep("masks", [M_COLS], BF16)
        rope_t = keep("rope_tables", [4, TT, HD])
        rowpar = keep("row_params", [512])
        ws_t = keep("gmlp_wT", [GG, P])
        R0 = place[0]
        act_hi = at("act_hi", [KD, SEQ], F32R, R0)
        act_lo = at("act_lo", [KD, SEQ], F32R, R0 + 8192)
        R1 = R0 + 16384
        end = R1 + 25600
        assert end <= nc.sbuf_usable_end, (end, nc.sbuf_usable_end)
        par_rows = at("par_rows", [P], F32, R1 + 8192)
        row_src = at("row_src", [512], F32, R1 + 8192 + 512)
        ws_in = at("gmlp_ws_in", [GG, P], F32, R1 + 8192 + 512 + 2048)
        xs = at("x_scaled", [TT, D], F32, R1)
        pqk = at("p_qk", [TT, 2 * QW], F32, R1)
        pv = at("p_v", [TT, QW], F32, R1 + 12288)
        uv = at("p_uv", [TT, 2 * GW], F32, R1 + 18432)
        tmp = at("rope_tmp", [2, QW // 2], F32, R1 + 22528)
        qT = at("qT", [6, SEQ], F32, R0)
        kT = at("kT", [6, SEQ], F32, R0 + 6144)
        cat_ab = at("cat_ab", [TT, 512], F32, R0 + 12288)
        cat_c = [at("cat_c0", [QW], F32, R0 + 12288), at("cat_c1", [QW], F32, R1 + 22528)]
        probs = at("probs", [2, 768], F32, R1)
        probs_t = at("probs_T", [2, 768], F32, R1 + 6144)
        conv_z = at("conv_z", [2, SEQ], F32, R1 + 18432)
        conv_y = at("conv_y", [2, SEQ], F32, R1 + 20480)
        conv_b = at("conv_b", [2, SEQ], F32, R0 - 2048)
        fh_hi = at("ffn_h_hi", [2, 4, SEQ], F32R, R1)
        fh_lo = at("ffn_h_lo", [2, 4, SEQ], F32R, R1 + 8192)
        fsg = at("ffn_silu", [2, SEQ], F32, R1 + 16384)
        fh = at("ffn_h", [2, SEQ], F32, R1 + 18432)
        xg_hi = at("xg_hi", [KD, P], F32R, R0)
        xg_lo = at("xg_lo", [KD, P], F32R, R0 + 4096)
        msg = at("moe_silu", [2, SLAB], F32, R0 + 8192)
        mh = at("moe_h", [2, SLAB], F32, R0 + 12288)
        mh_hi = at("moe_hT_hi", [4, P], F32R, R1)
        mh_lo = at("moe_hT_lo", [4, P], F32R, R1 + 2048)
        y_hi = at("moe_y_hi", [D], F32R, R1 + 4096)
        xs_hi = at("x_scaled_hi", [TT, D], F32R, R1 + 8192)
        y_lo = at("moe_y_lo", [D], F32R, R1 + 16384)
        pick = at("pick", [TT, P], F32R, R1 + 20480)
        pick_t = at("pick_T", [TT, P], F32R, R1 + 21504)
        rt = at("routing", [520], F32, R1 + 22528)

        ps = ctx.enter_context(nc.psum_tensor("psum", [P, 8, 512], F32))

        ident = cst[:, C_ID:C_ID + P]
        ones = cst[:, C_ONE:C_ONE + P]

        def sem(name):
            return ctx.enter_context(nc.semaphore(name))

        slot_loaded = [sem(f"slot_loaded{i}") for i in range(RING)]
        x_loaded, const_loaded, par_loaded = sem("x_loaded"), sem("const_loaded"), sem("par_loaded")
        rows_loaded, ws_loaded, router_loaded = sem("rows_loaded"), sem("ws_loaded"), sem("router_loaded")
        hi_ready, lo_ready, unit_used = sem("hi_ready"), sem("lo_ready"), sem("unit_used")
        dve_chain, act_chain, pool_chain = sem("dve_chain"), sem("act_chain"), sem("pool_chain")
        setup_pe, ws_masked, wsT_ready = sem("setup_pe"), sem("ws_masked"), sem("wsT_ready")
        col_ready, row_ready, rope_ready = sem("col_ready"), sem("row_ready"), sem("rope_ready")
        sq_act, ms_ready, std_ready, rstd_ready = sem("sq_act"), sem("ms_ready"), sem("std_ready"), sem("rstd_ready")
        xs_act, xs_dve = sem("xs_act"), sem("xs_dve")
        xt_done, xt_hi, xt_lo = sem("xt_done"), sem("xt_hi"), sem("xt_lo")
        proj_act, proj_dve = sem("proj_act"), sem("proj_dve")
        head_ms, head_std, head_rstd = sem("head_ms"), sem("head_std"), sem("head_rstd")
        q_roped, k_roped = sem("q_roped"), sem("k_roped")
        gv_ms, gv_std, gv_ready = sem("gv_ms"), sem("gv_std"), sem("gv_ready")
        router_hi_ready, router_lo_ready = sem("router_hi_ready"), sem("router_lo_ready")
        xs_hi_ready, xs_lo_ready, masks_loaded = sem("xs_hi_ready"), sem("xs_lo_ready"), sem("masks_loaded")
        qkT_done, qkT_act, qkT_dve = sem("qkT_done"), sem("qkT_act"), sem("qkT_dve")
        gy_done, gcat_ready = sem("gy_done"), sem("gcat_ready")
        s_done, max_ready, p_ready = sem("scores_done"), sem("max_ready"), sem("probs_ready")
        pT_done, pT_ready, o_done, o_ready = sem("probsT_done"), sem("probsT_ready"), sem("o_done"), sem("o_ready")
        ct_done, ct_hi, ct_lo = sem("catT_done"), sem("catT_hi"), sem("catT_lo")
        res_added = sem("residual_added")
        fsg_ready, fh_ready, fh_hi_ready, fh_lo_ready = (
            sem("ffn_silu_ready"), sem("ffn_h_ready"), sem("ffn_h_hi"), sem("ffn_h_lo"))
        cv_copied, cv_z, cv_ready = sem("conv_copied"), sem("conv_z_ready"), sem("conv_ready")
        lg_done, diff_ready, exp_ready, sel_ready = sem("logits_done"), sem("diff_ready"), sem("exp_ready"), sem("sel_ready")
        cnt_done, meta_ready = sem("counts_done"), sem("meta_ready")
        pick_ready, gather_done, xg_hi_ready, xg_lo_ready = (
            sem("pick_ready"), sem("gather_done"), sem("xg_hi_ready"), sem("xg_lo_ready"))
        silu_ready, h_ready = sem("silu_ready"), sem("h_ready")
        hT_done, hT_hi, hT_lo = sem("hT_done"), sem("hT_hi"), sem("hT_lo")
        y_zeroed, y_act, y_dve = sem("y_zeroed"), sem("y_act"), sem("y_dve")
        comb_done, comb_added = sem("combine_done"), sem("combine_added")
        pickT_done, pickT_ready, zeroed = sem("pickT_done"), sem("pickT_ready"), sem("zeroed")
        out_stored = sem("out_stored")

        SS, MS, SD, RS = 0, 2, 4, 6
        HSS, HMS, HSD, HRS, HN = 16, 72, 128, 184, 56
        MX, NM, LS, RL = 240, 264, 288, 312

        def head_sums(at_, which, t):
            c = at_ + 8 + (which * TT + t) * HEADS
            return small[:, c:c + HEADS]

        T_SEL, T_RANK, T_GATE, T_LG, T_MX, T_DIFF, T_EXP, T_G1, T_G2, T_DEN = 0, 16, 32, 48, 64, 80, 82, 84, 86, 88
        T_TMP, T_POS, T_OVER, T_OIDX, T_W, T_Q, T_JP, T_JG = 96, 112, 136, 144, 152, 176, 192, 216
        T_F, T_JUNK, T_CMP, T_CMP2 = 240, 248, 256, 384
        T_GTOK, T_GSLOT = 512, 514

        def bank(b, cols=512):
            return ps[:, b, 0:cols]

        def raw_unit(u):
            t, r0, n, c0, w = units[u]
            _, nrow, ncol = tiles[t]
            full = raw[:, t % RING, 0:nrow * ncol].rearrange("p (k f) -> p k f", f=ncol)
            return full[:, r0:r0 + n, c0:c0 + w]

        def part(buf, u, w):
            return buf[:, u % SPLITS, :].rearrange("p (k f) -> p k f", f=w)

        def split_hi(act, u):
            if u >= U_MOE:
                return
            t, w = units[u][0], units[u][4]
            act.wait_ge(slot_loaded[t % RING], 16 * (t // RING + 1))
            if u >= SPLITS:
                act.wait_ge(unit_used, u - SPLITS + 1)
            act.activation(part(wh, u, w), raw_unit(u), ACT.Copy).then_inc(hi_ready, 1)

        def split_lo(dve, u):
            if u >= U_MOE:
                return
            w = units[u][4]
            dve.wait_ge(hi_ready, u + 1)
            dve.tensor_tensor(part(wl, u, w), raw_unit(u), part(wh, u, w).bitcast(F32),
                              ALU.subtract).then_inc(lo_ready, 1)

        def moe_raw(i, q):
            return raw[:, i % RING, q * UNIT:(q + 1) * UNIT]

        def moe_split_hi(act, j, v):
            i, q = divmod(v, TILE // UNIT)
            if q == 0:
                act.wait_ge(slot_loaded[i % RING],
                            16 * (T_MOE // RING + i // RING + 1) + j * (16 * JOB_TILES // RING))
            act.wait_ge(unit_used, j * JOB_UNITS + (U_MOE + v - SPLITS + 1))
            act.activation(wh[:, v % SPLITS, :], moe_raw(i, q), ACT.Copy).then_inc(hi_ready, 1)

        def moe_split_lo(dve, j, v):
            i, q = divmod(v, TILE // UNIT)
            dve.wait_ge(hi_ready, j * JOB_UNITS + (U_MOE + v + 1))
            dve.tensor_tensor(wl[:, v % SPLITS, :], moe_raw(i, q), wh[:, v % SPLITS, :].bitcast(F32),
                              ALU.subtract).then_inc(lo_ready, 1)

        job_steps = [("g", 0), ("u", 0)]
        for i in range(1, SLABS):
            job_steps += [("g", i), ("u", i), ("d", i - 1)]
        job_steps += [("d", SLABS - 1)]

        ROPE_HEADS = 3
        ROPE_PARTS = TT * HEADS // ROPE_HEADS

        def rope_part(eng, link, scratch, which, part_, roped):
            n = ROPE_HEADS
            w = n * HD
            t, h0 = divmod(part_ * n, HEADS)
            c0 = which * QW + h0 * HD
            v = pqk[:, t, c0:c0 + w].rearrange("p (h d) -> p h d", d=HD)
            t1 = scratch[:, 0:w].rearrange("p (h d) -> p h d", d=HD)
            t2 = scratch[:, w:2 * w].rearrange("p (h d) -> p h d", d=HD)
            cos = rope_t[:, 2 * which, t, :]
            sin = rope_t[:, 2 * which + 1, t, :]
            eng.tensor_tensor(t1, v, cos.unsqueeze(1).broadcast_to([P, n, HD]), ALU.mult)
            for a, b in ((0, HH), (HH, 0)):
                ins = eng.tensor_tensor(t2[:, :, a:a + HH], v[:, :, b:b + HH],
                                        sin[:, a:a + HH].unsqueeze(1).broadcast_to([P, n, HH]), ALU.mult)
            link(ins)
            link(eng.tensor_tensor(t1, t1, t2, ALU.add))
            rs = head_sums(HRS, which, t)[:, h0:h0 + n]
            ins = eng.tensor_tensor(v, t1, rs.unsqueeze(2).broadcast_to([P, n, HD]), ALU.mult)
            if part_ == ROPE_PARTS - 1:
                ins.then_inc(roped, 1)
            else:
                link(ins)

        heads_of = [[(n // 4, [g * 4 + n % 4 for g in range(3)]) for n in range(8)],
                    [(n // 4, [6 * (n % 4 // 2) + n % 2 + 2 * g for g in range(3)]) for n in range(8)]]
        sc_banks = [2, 0]

        def scores_psum(n, seg, keys):
            flat = ps[:, sc_banks[n % 2]:sc_banks[n % 2] + 2, :].rearrange("p b f -> p (b f)")
            return flat[:, seg * 256:seg * 256 + keys]

        def scores_psum_all(n, keys):
            flat = ps[:, sc_banks[n % 2]:sc_banks[n % 2] + 2, :].rearrange("p b f -> p (b f)")
            return flat[:, 0:768].rearrange("p (s k) -> p s k", s=3)[:, :, 0:keys]

        col_tiles = ((0, 1, 2, "g", 3, 4), (0, 1, 2, 3, 4))
        read_act = ((1, 2, 3, 4, 5, 6), (7, 8, 9, 10, 11))
        read_dve = ((1, 2, 3, 3, 4, 5), (6, 7, 8, 9, 10))
        gain_rows = (R_MIX, R_FFN, R_MIX + KD, R_FFN + KD)
        nblk = sum(w // P for w in widths)
        block_slab = [s for s, w in enumerate(widths) for _ in range(w // P)]
        block_first = [sum(w // P for w in widths[:s]) for s in range(len(widths))]

        block = ctx.enter_context(nc.Block())

        @block.sync
        def _(sp):
            sp.dma_start(xres[:, :, :], x[0].rearrange("(t p) d -> p t d", p=P)).then_inc(x_loaded, 16)
            sp.dma_start(cst[:, :], const_f32).then_inc(const_loaded, 16)
            sp.dma_start(par_rows[R_MIX:R_MIX + 16, :], norm_mix.rearrange("l (k p) -> (l k) p", p=P)).then_inc(par_loaded, 16)
            sp.dma_start(par_rows[R_FFN:R_FFN + 16, :], norm_ffn.rearrange("l (k p) -> (l k) p", p=P)).then_inc(par_loaded, 16)
            sp.dma_start(par_rows[R_BS:R_BS + 4, :], gmlp_bs[0]).then_inc(par_loaded, 16)
            sp.dma_start(par_rows[R_CONV:R_CONV + 6, :], conv_w[0].rearrange("t (k p) -> (t k) p", p=P)).then_inc(par_loaded, 16)
            for src, at_, n in ((dil_q_gain, B_DQ, HD), (dil_k_gain, B_DK, HD), (moba_q_gain, B_MQ, HD),
                                (moba_k_gain, B_MK, HD), (gmlp_v_gain, B_GV, GW)):
                sp.dma_start(row_src[0:1, at_:at_ + n], src).then_inc(rows_loaded, 16)
            sp.dma_start(ws_in[:, :, :], gmlp_ws[0].rearrange("g i j -> i g j")).then_inc(ws_loaded, 16)
            for t, (src, nrow, ncol) in enumerate(tiles):
                if t >= RING:
                    sp.wait_ge(lo_ready, tile_last[t - RING] + 1)
                dst = raw[:, t % RING, 0:nrow * ncol].rearrange("p (k f) -> p k f", f=ncol)
                sp.dma_start(dst, src).then_inc(slot_loaded[t % RING], 16)
                if t == RING - 1:
                    sp.dma_start(router[:, :, :], router_w[0].rearrange("(k p) e -> p k e", p=P)).then_inc(router_loaded, 16)

            def job_loads(e, j, static_first):
                for i, (kind, s) in enumerate(job_steps):
                    if static_first and i < RING:
                        sp.wait_ge(lo_ready, tile_last[T_MOE - RING + i] + 1)
                    else:
                        sp.wait_ge(lo_ready, j * JOB_UNITS + (U_MOE + (i - RING + 1) * (TILE // UNIT)))
                    if kind == "d":
                        src = moe_w_down[0, e, s * SLAB:(s + 1) * SLAB, :]
                        dst = raw[:, i % RING, :].rearrange("p (k f) -> p k f", k=4)
                    else:
                        w = moe_w_gate if kind == "g" else moe_w_up
                        src = w[0, e, :, s * SLAB:(s + 1) * SLAB]
                        dst = raw[:, i % RING, :].rearrange("p (k f) -> p k f", k=KD)
                    if len(src.shape) == 3:
                        src = src.rearrange("o (k p) f -> p (o k) f", p=P)
                    else:
                        src = src.rearrange("(k p) f -> p k f", p=P)
                    sp.dma_start(dst, src).then_inc(slot_loaded[i % RING], 16)

            job_loads(0, 0, True)
            with sp.Fori(1, NE - 1) as j:
                job_loads(bass.ds(j, 1), j, False)
            sp.wait_ge(meta_ready, 1)
            jobs = sp.value_load(meta[0:1, 0:1], min_val=NE, max_val=JOBS_MAX)
            with sp.Fori(NE - 1, jobs) as j:
                e = sp.value_load(meta[0:1, bass.ds(j - (NE - 2), 1)], min_val=0, max_val=NE - 1)
                job_loads(bass.ds(e, 1), j, False)
            sp.wait_ge(comb_added, jobs + 1)
            sp.dma_start(out[0].rearrange("(t p) d -> p t d", p=P), xres[:, :, :]).then_inc(out_stored, 16)
            sp.wait_ge(out_stored, 16)

        @block.gpsimd
        def _(pool):
            pool.dma_start(msk[:, :], const_mask).then_inc(masks_loaded, 16)
            pool.wait_ge(ws_loaded, 16)
            pool.affine_select(out=ws_in[:, :, :], in_=ws_in[:, :, :], compare_op=ALU.is_ge, fill=0.0, base=0,
                               pattern=[[0, GG], [-1, P]], channel_multiplier=1).then_inc(ws_masked, 1)

            n = [0]

            def step(ins):
                n[0] += 1
                ins.then_inc(pool_chain, 1)
                pool.wait_ge(pool_chain, n[0])

            def rope_k(layer):
                pool.wait_ge(head_rstd, layer + 1)
                pool.wait_ge(rope_ready, layer + 1)
                for part_ in range(ROPE_PARTS):
                    rope_part(pool, step, tmp[:, 1, :], 1, part_, k_roped)

            def rope_tables(gq, gk):
                for n, g in enumerate((gq, gk)):
                    gain = rowpar[:, g:g + HD]
                    for half in range(2):
                        lo = half * HH
                        hi = HH - lo
                        last = pool.tensor_tensor(
                            rope_t[:, 2 * n + 1, :, lo:lo + HH],
                            cst[:, C_SIN:C_SIN + TT * HD].rearrange("p (t d) -> p t d", t=TT)[:, :, lo:lo + HH],
                            gain[:, hi:hi + HH].unsqueeze(1).broadcast_to([P, TT, HH]), ALU.mult)
                    last = pool.tensor_tensor(
                        rope_t[:, 2 * n, :, :],
                        cst[:, C_COS:C_COS + TT * HD].rearrange("p (t d) -> p t d", t=TT),
                        gain.unsqueeze(1).broadcast_to([P, TT, HD]), ALU.mult)
                last.then_inc(rope_ready, 1)

            pool.wait_ge(row_ready, 1)
            pool.wait_ge(const_loaded, 16)
            rope_tables(B_DQ, B_DK)
            rope_k(0)
            pool.wait_ge(q_roped, 1)
            pool.wait_ge(k_roped, 1)
            rope_tables(B_MQ, B_MK)
            rope_k(1)


            pool.wait_ge(cv_z, 1)
            pool.wait_ge(cv_copied, 2)
            conv_s = rowpar[:, B_GV:B_GV + SEQ]
            taps = [colpar[:, R_CONV + 2 * t:R_CONV + 2 * t + 2] for t in range(3)]
            for c in range(2):
                step(pool.tensor_scalar(conv_y[:, c, :], conv_z[:, c, :], taps[2][:, c:c + 1], None, ALU.mult))
            for back in (1, 2):
                for c in range(2):
                    step(pool.tensor_scalar(conv_s[:, 0:SEQ - back], conv_z[:, c, 0:SEQ - back],
                                            taps[2 - back][:, c:c + 1], None, ALU.mult))
                    step(pool.tensor_tensor(conv_y[:, c, back:SEQ], conv_y[:, c, back:SEQ],
                                            conv_s[:, 0:SEQ - back], ALU.add))
            pool.tensor_tensor(conv_y[:, :, :], conv_y[:, :, :], conv_b[:, :, :], ALU.mult).then_inc(cv_ready, 1)

            pool.wait_ge(ct_lo, 6)
            pool.memset(rt[:, T_GSLOT:T_GSLOT + 1], 0.0)
            pool.memset(rt[:, T_JP:T_JP + TT * JCOLS], -1.0)
            pool.memset(rt[:, T_JG:T_JG + TT * JCOLS], 0.0).then_inc(zeroed, 1)
            pool.memset(pick_t[:, :, :].bitcast(F32), 0.0)
            pool.wait_ge(xs_lo_ready, 1)
            for t in (y_hi[:, :], y_lo[:, :]):
                ins = pool.memset(t.bitcast(F32), 0.0)
            ins.then_inc(zeroed, 1)

        @block.tensor
        def _(pe):
            def three(out_, sh, sl, mh_, ml_, start, stop):
                pe.matmul(out_, sh, mh_, start=start, stop=False)
                pe.matmul(out_, sh, ml_, start=False, stop=False)
                return pe.matmul(out_, sl, mh_, start=False, stop=stop)

            def setup():
                pe.wait_ge(const_loaded, 16)
                pe.wait_ge(par_loaded, 64)
                pe.transpose(ps[:, 0, 0:R_ROWS], par_rows[0:R_ROWS, :], cst[0:R_ROWS, 0:R_ROWS]).then_inc(setup_pe, 1)

            def setup_rows():
                pe.wait_ge(rows_loaded, 80)
                pe.matmul(bank(3), cst[0:1, C_ONE:C_ONE + P], row_src[0:1, :], start=True, stop=True).then_inc(setup_pe, 1)

            def setup_ws():
                pe.wait_ge(ws_masked, 1)
                for g in range(GG):
                    mm = pe.transpose(ps[:, 2, g * P:(g + 1) * P], ws_in[:, g, :], ident)
                mm.then_inc(setup_pe, 1)

            def norm_T(n):
                for q in range(4):
                    pe.wait_ge(xs_act, 2 * n + q // 2 + 1)
                    pe.wait_ge(xs_dve, 2 * n + q // 2 + 1)
                    for kk in range(2):
                        for t in range(TT):
                            k = 2 * q + kk
                            mm = pe.transpose(ps[:, 4 + q, (kk * TT + t) * P:(kk * TT + t + 1) * P],
                                              xs[:, t, k * P:(k + 1) * P], ident)
                    mm.then_inc(xt_done, 1)

            def project(u0, u1, layer):
                u, c = u0, 0
                while u < u1:
                    t = units[u][0]
                    ncol = tiles[t][2]
                    b = (c % 2) * 2
                    if c == 1 and layer == 0:
                        pe.wait_ge(wsT_ready, 1)
                        pe.wait_ge(row_ready, 1)
                    if c >= 2:
                        pe.wait_ge(proj_act, read_act[layer][c - 2])
                        pe.wait_ge(proj_dve, read_dve[layer][c - 2])
                    while u < u1 and units[u][0] == t:
                        _, r0, n, _, w = units[u]
                        pe.wait_ge(lo_ready, u + 1)
                        for r in range(n):
                            k = r0 + r
                            if c == 0 and k % 2 == 0:
                                pe.wait_ge(xt_lo, 8 * layer + k // 2 + 1)
                            for tt in range(TT):
                                sl = slice(tt * P, tt * P + P)
                                mm = three(ps[:, b + tt, 0:ncol], act_hi[:, k, sl], act_lo[:, k, sl],
                                           part(wh, u, w)[:, r, :], part(wl, u, w)[:, r, :], k == 0, k == KD - 1)
                        mm.then_inc(unit_used, 1)
                        u += 1
                    c += 1

            def heads_T(layer):
                pe.wait_ge(q_roped, layer + 1)
                for r in range(6):
                    if r == 3:
                        pe.wait_ge(k_roped, layer + 1)
                    if r == 4:
                        pe.wait_ge(proj_act, (6, 11)[layer])
                        pe.wait_ge(proj_dve, (5, 10)[layer])
                    which, b0 = divmod(r, 3)
                    for bb in range(2):
                        for t in range(TT):
                            blk = 2 * b0 + bb
                            c0 = which * QW + blk * P
                            mm = pe.transpose(ps[:, (4 + r) % 8, (bb * TT + t) * P:(bb * TT + t + 1) * P],
                                              pqk[:, t, c0:c0 + P], ident)
                    mm.then_inc(qkT_done, 1)

            def gmlp():
                pe.wait_ge(gv_ready, 1)
                pe.wait_ge(wsT_ready, 1)
                pe.wait_ge(qkT_dve, 3)
                pe.wait_ge(qkT_act, 3)
                for t in range(TT):
                    for g in range(GG):
                        c = (t * GG + g) * HD
                        mm = pe.matmul(ps[:, 6, c:c + HD], ws_t[:, g, :], uv[:, t, GW + g * HD:GW + (g + 1) * HD],
                                       start=True, stop=True)
                mm.then_inc(gy_done, 1)

            def attention(layer):
                items = heads_of[layer]
                o0 = 8 * layer
                for n in range(10):
                    if n < 8:
                        tt, hs = items[n]
                        keys = P * (tt + 1)
                        if n == 0:
                            pe.wait_ge(qkT_act, 3 * layer + 3)
                            pe.wait_ge(qkT_dve, 3 * layer + 3)
                        if n >= 2:
                            pe.wait_ge(max_ready, o0 + n - 1)
                        for seg, h in enumerate(hs):
                            lo = (h % 2) * HD
                            mm = pe.matmul(scores_psum(n, seg, keys), qT[lo:lo + HD, h // 2, tt * P:(tt + 1) * P],
                                           kT[lo:lo + HD, h // 2, 0:keys], start=True, stop=True)
                        mm.then_inc(s_done, 1)
                        if n == 0 and layer == 0:
                            gmlp()
                    if 1 <= n <= 8:
                        m = n - 1
                        tt, hs = items[m]
                        pe.wait_ge(p_ready, o0 + m + 1)
                        if m >= 1:
                            pe.wait_ge(pT_ready, o0 + m)
                        nb = 3 * (tt + 1)
                        for b in range(nb):
                            mm = pe.transpose(ps[:, 4 + b // 4, (b % 4) * P:(b % 4 + 1) * P],
                                              probs[:, m % 2, b * P:(b + 1) * P], ident)
                        mm.then_inc(pT_done, 1)
                    if n >= 2:
                        m = n - 2
                        tt, hs = items[m]
                        pe.wait_ge(pT_ready, o0 + m + 1)
                        if m >= 2:
                            pe.wait_ge(o_ready, o0 + m - 1)
                        if m == 1 and layer == 0:
                            pe.wait_ge(gcat_ready, 1)
                        for seg, h in enumerate(hs):
                            for kb in range(tt + 1):
                                b = seg * (tt + 1) + kb
                                if layer == 0:
                                    o = ps[:, 7 - m % 2, 0:HD]
                                    st, sp_ = b == 0, b == 3 * (tt + 1) - 1
                                else:
                                    o = ps[:, 7 - m % 2, seg * HD:(seg + 1) * HD]
                                    st, sp_ = kb == 0, kb == tt
                                mm = pe.matmul(o, probs_t[:, m % 2, b * P:(b + 1) * P],
                                               pv[:, kb, h * HD:(h + 1) * HD], start=st, stop=sp_)
                        mm.then_inc(o_done, 1)

            def cat_T(layer):
                pe.wait_ge(o_ready, 8 * (layer + 1))
                pe.wait_ge(max_ready, 8 * (layer + 1))
                for r in range(2 + layer):
                    for bb in range(2):
                        for t in range(TT):
                            blk = 2 * r + bb
                            src = cat_ab[:, t, blk * P:(blk + 1) * P] if layer == 0 else cat_c[t][:, blk * P:(blk + 1) * P]
                            mm = pe.transpose(ps[:, r, (bb * TT + t) * P:(bb * TT + t + 1) * P], src, ident)
                    mm.then_inc(ct_done, 1)

            def out_projection(layer):
                u0, u1 = (first["out_ab"], first["ffn"]) if layer == 0 else (first["out_cd"], first["moe"])
                pe.wait_ge(ct_lo, (2, 6)[layer])
                pe.wait_ge(pT_ready, 8 * (layer + 1))
                for u in range(u0, u1):
                    k = u - u0
                    pe.wait_ge(lo_ready, u + 1)
                    for tt in range(TT):
                        for half in range(2):
                            cs = slice(half * 512, half * 512 + 512)
                            sl = slice(tt * P, tt * P + P)
                            mm = three(bank(4 + 2 * tt + half), act_hi[:, k, sl], act_lo[:, k, sl],
                                       wh[:, u % SPLITS, cs], wl[:, u % SPLITS, cs], k == 0, u == u1 - 1)
                    mm.then_inc(unit_used, 1)

            def ffn():
                u = first["ffn"]
                for s in range(len(widths) + 1):
                    if s < len(widths):
                        for bb in range(widths[s] // P):
                            b = block_first[s] + bb
                            if b >= 4:
                                pe.wait_ge(fh_ready, b - 3)
                            for which in range(2):
                                pe.wait_ge(lo_ready, u + 1)
                                o = ps[:, b % 4, which * SEQ:(which + 1) * SEQ]
                                for k in range(KD):
                                    if b == 0 and which == 0 and k % 2 == 0:
                                        pe.wait_ge(xt_lo, 4 + k // 2 + 1)
                                    mm = three(o, part(wh, u, P)[:, k, :], part(wl, u, P)[:, k, :],
                                               act_hi[:, k, :], act_lo[:, k, :], k == 0, k == KD - 1)
                                mm.then_inc(unit_used, 1)
                                u += 1
                    if s >= 1:
                        for c in range(widths[s - 1] // P):
                            b = block_first[s - 1] + c
                            pe.wait_ge(fh_lo_ready, b + 1)
                            pe.wait_ge(lo_ready, u + 1)
                            for tt in range(TT):
                                for half in range(2):
                                    cs = slice(half * 512, half * 512 + 512)
                                    sl = slice(tt * P, tt * P + P)
                                    mm = three(bank(4 + 2 * tt + half), fh_hi[:, (s - 1) % 2, c, sl],
                                               fh_lo[:, (s - 1) % 2, c, sl], wh[:, u % SPLITS, cs],
                                               wl[:, u % SPLITS, cs], b == 0, b == nblk - 1)
                            mm.then_inc(unit_used, 1)
                            u += 1

            def conv_projection():
                for z in range(3):
                    for c in range(2):
                        u = first["conv"] + 2 * z + c
                        pe.wait_ge(lo_ready, u + 1)
                        o = ps[:, 4 + z, c * SEQ:(c + 1) * SEQ]
                        for k in range(KD):
                            mm = three(o, part(wh, u, P)[:, k, :], part(wl, u, P)[:, k, :],
                                       act_hi[:, k, :], act_lo[:, k, :], k == 0, k == KD - 1)
                        mm.then_inc(unit_used, 1)

            setup()
            norm_T(0)
            setup_rows()
            setup_ws()
            project(0, first["out_ab"], 0)
            heads_T(0)
            attention(0)
            cat_T(0)
            out_projection(0)
            norm_T(1)
            ffn()
            norm_T(2)
            project(first["in_cd"], first["conv"], 1)
            conv_projection()
            pe.wait_ge(cv_copied, 2)
            pe.wait_ge(cv_z, 1)
            heads_T(1)
            attention(1)
            cat_T(1)
            out_projection(1)
            norm_T(3)
            pe.wait_ge(router_lo_ready, 1)
            for tt in range(TT):
                for k in range(KD):
                    if tt == 0 and k % 2 == 0:
                        pe.wait_ge(xt_lo, 12 + k // 2 + 1)
                    sl = slice(tt * P, tt * P + P)
                    mm = three(ps[:, 0, tt * NE:(tt + 1) * NE], act_hi[:, k, sl], act_lo[:, k, sl],
                               router_hi[:, k, :], router_lo[:, k, :], k == 0, k == KD - 1)
            mm.then_inc(lg_done, 1)
            pe.wait_ge(sel_ready, 1)
            sel = [rt[:, T_SEL + t * NE:T_SEL + (t + 1) * NE] for t in range(TT)]
            up = cst[:, C_UP:C_UP + P]
            pe.matmul(ps[:, 1, 0:8], up, sel[0], start=True, stop=True)
            pe.matmul(ps[:, 1, 8:16], ones, sel[0], start=True, stop=False)
            pe.matmul(ps[:, 1, 8:16], up, sel[1], start=False, stop=True)
            pe.matmul(ps[:, 1, 16:24], ones, sel[0], start=True, stop=False)
            pe.matmul(ps[:, 1, 16:24], ones, sel[1], start=False, stop=True).then_inc(cnt_done, 1)

            def gather(j1):
                pe.wait_ge(pick_ready, j1 + 1)
                for k in range(KD):
                    o = ps[:, 1 if k < 4 else 3, (k % 4) * P:(k % 4 + 1) * P]
                    for t in range(TT):
                        pe.matmul(o, xs_hi[:, t, k * P:(k + 1) * P], pick[:, t, :], start=t == 0, stop=False)
                        mm = pe.matmul(o, xs_lo[:, t, k * P:(k + 1) * P], pick[:, t, :], start=False, stop=t == TT - 1)
                    if k % 4 == 3:
                        mm.then_inc(gather_done, 1)

            def combine(j):
                pe.wait_ge(y_dve, j + 1)
                pe.wait_ge(xg_lo_ready, 2 * j + 2)
                for n, b in enumerate((5, 4, 3, 1)):
                    t, half = divmod(n, 2)
                    cs = slice(half * 512, half * 512 + 512)
                    pe.matmul(bank(b), pick_t[:, t, :], y_hi[:, cs], start=True, stop=False)
                    mm = pe.matmul(bank(b), pick_t[:, t, :], y_lo[:, cs], start=False, stop=True)
                mm.then_inc(comb_done, 1)

            def transpose_h(j, i):
                pe.wait_ge(h_ready, SLABS * j + (i + 1))
                if i >= 1:
                    pe.wait_ge(hT_lo, SLABS * j + i)
                for c in range(4):
                    mm = pe.transpose(ps[:, 4, c * P:(c + 1) * P], mh[:, i % 2, c * P:(c + 1) * P], ident)
                mm.then_inc(hT_done, 1)

            pe.wait_ge(xs_lo_ready, 1)
            gather(0)
            pe.wait_ge(zeroed, 2)
            for half in range(2):
                mm = pe.matmul(bank(6 + half), pick_t[:, 0, :], y_hi[:, 0:512], start=True, stop=True)
            mm.then_inc(y_zeroed, 1)
            pe.wait_ge(meta_ready, 1)
            jobs = pe.value_load(meta[0:1, 0:1], min_val=NE, max_val=JOBS_MAX)
            with pe.Fori(0, jobs) as j:
                for v, (kind, i) in enumerate(job_steps):
                    if kind == "g" and i == 1:
                        pe.wait_ge(comb_added, j + 1)
                    if kind == "g" and i >= 2:
                        pe.wait_ge(silu_ready, SLABS * j + (i - 1))
                    if kind == "u" and i >= 2:
                        pe.wait_ge(h_ready, SLABS * j + (i - 1))
                    if kind == "d" and i == 0:
                        pe.wait_ge(y_dve, j + 1)
                    if kind == "d":
                        pe.wait_ge(hT_lo, SLABS * j + (i + 1))
                    for q in range(4):
                        w = 4 * v + q
                        pe.wait_ge(lo_ready, j * JOB_UNITS + (U_MOE + w + 1))
                        if v == 0 and q % 2 == 0:
                            pe.wait_ge(xg_lo_ready, 2 * j + (q // 2 + 1))
                        if kind == "d":
                            for half in range(2):
                                cs = slice(half * 512, half * 512 + 512)
                                mm = three(bank(6 + half), mh_hi[:, q, :], mh_lo[:, q, :], wh[:, w % SPLITS, cs],
                                           wl[:, w % SPLITS, cs], i == 0 and q == 0, i == SLABS - 1 and q == 3)
                        else:
                            b = (0 if kind == "g" else 2) + i % 2
                            for r in range(2):
                                k = 2 * q + r
                                cs = slice(r * 512, r * 512 + 512)
                                mm = three(bank(b), xg_hi[:, k, :], xg_lo[:, k, :], wh[:, w % SPLITS, cs],
                                           wl[:, w % SPLITS, cs], k == 0, k == KD - 1)
                        mm.then_inc(unit_used, 1)
                    if kind == "g" and i == 0:
                        combine(j)
                    if kind == "g" and i >= 1:
                        transpose_h(j, i - 1)
                    if kind == "g" and i == 2:
                        for t in range(TT):
                            pe.transpose(ps[:, 5, t * P:(t + 1) * P], pick[:, t, :].bitcast(F32), ident)
                        for t in range(TT):
                            mm = pe.matmul(ps[:, 5, TT * P:TT * P + 1], pick[:, t, :].bitcast(F32),
                                           rt[:, T_GTOK + t:T_GTOK + t + 1], start=t == 0, stop=t == TT - 1)
                        mm.then_inc(pickT_done, 1)
                    if kind == "d" and i == SLABS - 2:
                        transpose_h(j, SLABS - 1)
                        gather(j + 1)
            combine(jobs)

        @block.scalar
        def _(act):
            def norm(n):
                act.preload_act_table(ACT.Sqrt)
                if n == 0:
                    act.wait_ge(x_loaded, 16)
                else:
                    act.wait_ge(res_added, n)
                act.activation(xs[:, 0, :], xres[:, 0, :], ACT.Square, accum_out=small[:, SS:SS + 1]).then_inc(sq_act, 1)
                act.wait_ge(ms_ready, n + 1)
                act.activation(small[:, SD:SD + 2], small[:, MS:MS + 2], ACT.Sqrt).then_inc(std_ready, 1)
                act.wait_ge(rstd_ready, n + 1)
                for half in range(2):
                    cs = slice(half * 512, half * 512 + 512)
                    act.activation(xs[:, 0, cs], xres[:, 0, cs], ACT.Copy, scale=small[:, RS:RS + 1]).then_inc(xs_act, 1)
                if n == 0:
                    for u in range(SPLITS):
                        split_hi(act, u)
                    act.wait_ge(col_ready, 1)
                for q in range(4):
                    act.wait_ge(xt_done, 4 * n + q + 1)
                    for kk in range(2):
                        k = 2 * q + kk
                        g = gain_rows[n] + k
                        ins = act.activation(act_hi[:, k, :], ps[:, 4 + q, kk * SEQ:(kk + 1) * SEQ], ACT.Copy,
                                             scale=colpar[:, g:g + 1])
                    ins.then_inc(xt_hi, 1)

            def project(u0, u1, layer):
                u, c = u0, 0
                while u < u1:
                    t = units[u][0]
                    ncol = tiles[t][2]
                    b = (c % 2) * 2
                    while u < u1 and units[u][0] == t:
                        split_hi(act, u + SPLITS)
                        u += 1
                    act.wait_ge(unit_used, u)
                    m = col_tiles[layer][c]
                    if m == "g":
                        act.activation(uv[:, 0, :], bank(b), ACT.Gelu_apprx_tanh)
                        act.activation(uv[:, 1, :], bank(b + 1), ACT.Gelu_apprx_tanh).then_inc(proj_act, 1)
                    else:
                        dst = pqk[:, 0, m * 512:m * 512 + ncol] if m < 3 else pv[:, 0, (m - 3) * 512:(m - 3) * 512 + ncol]
                        act.activation(dst, bank(b, ncol), ACT.Copy).then_inc(proj_act, 1)
                    if m == 2:
                        act.wait_ge(head_ms, layer + 1)
                        act.activation(small[:, HSD + 8:HSD + HN], small[:, HMS + 8:HMS + HN],
                                       ACT.Sqrt).then_inc(head_std, 1)
                        act.preload_act_table(ACT.Exp if layer else ACT.Gelu_apprx_tanh)
                    if m == 3 and layer == 0:
                        act.wait_ge(gv_ms, 1)
                        act.activation(small[:, HSD:HSD + 8], small[:, HMS:HMS + 8], ACT.Sqrt).then_inc(gv_std, 1)
                        act.preload_act_table(ACT.Exp)
                    c += 1

            def heads_T(layer):
                for r in (0, 2, 4):
                    act.wait_ge(qkT_done, 6 * layer + r + 1)
                    dst = qT if r < 3 else kT
                    act.activation(dst[:, 2 * (r % 3):2 * (r % 3) + 2, :],
                                   ps[:, (4 + r) % 8, :].rearrange("p (b f) -> p b f", b=2), ACT.Copy).then_inc(qkT_act, 1)

            def attention(layer):
                o0 = 8 * layer
                for n in range(9):
                    if n < 8:
                        tt, hs = heads_of[layer][n]
                        keys = P * (tt + 1)
                        act.wait_ge(max_ready, o0 + n + 1)
                        for seg in range(3 if layer else 1):
                            w = keys if layer else 3 * keys
                            v = probs[:, n % 2, seg * w:(seg + 1) * w]
                            c = 3 * n + seg
                            ins = act.activation(v, v, ACT.Exp, bias=small[:, NM + c:NM + c + 1],
                                                 accum_out=small[:, LS + c:LS + c + 1])
                        ins.then_inc(p_ready, 1)
                    if n >= 1:
                        m = n - 1
                        nb = 3 * (heads_of[layer][m][0] + 1)
                        act.wait_ge(pT_done, o0 + m + 1)
                        if m >= 2:
                            act.wait_ge(o_done, o0 + m - 1)
                        act.activation(probs_t[:, m % 2, 0:nb * P],
                                       ps[:, 4:6, :].rearrange("p b f -> p (b f)")[:, 0:nb * P],
                                       ACT.Copy).then_inc(pT_ready, 1)

            def cat_T(layer):
                for r in range(2 + layer):
                    act.wait_ge(ct_done, 2 * layer + r + 1)
                    act.activation(act_hi[:, 2 * r:2 * r + 2, :],
                                   ps[:, r, :].rearrange("p (b f) -> p b f", b=2), ACT.Copy).then_inc(ct_hi, 1)
                if layer == 1:
                    act.wait_ge(cv_ready, 1)
                    act.activation(act_hi[:, 6:8, :], conv_y[:, :, :], ACT.Copy).then_inc(ct_hi, 1)

            def ffn():
                u = first["ffn"]
                for s in range(len(widths) + 1):
                    if s < len(widths):
                        for bb in range(widths[s] // P):
                            b = block_first[s] + bb
                            split_hi(act, u + SPLITS)
                            split_hi(act, u + 1 + SPLITS)
                            u += 2
                            act.wait_ge(unit_used, u)
                            if b >= 2:
                                act.wait_ge(fh_ready, b - 1)
                            act.activation(fsg[:, b % 2, :], ps[:, b % 4, 0:SEQ], ACT.Silu).then_inc(fsg_ready, 1)
                            act.wait_ge(fh_ready, b + 1)
                            act.activation(fh_hi[:, s % 2, bb, :], fh[:, b % 2, :], ACT.Copy).then_inc(fh_hi_ready, 1)
                    if s >= 1:
                        for c in range(widths[s - 1] // P):
                            split_hi(act, u + SPLITS)
                            u += 1

            norm(0)
            act.wait_ge(setup_pe, 3)
            act.activation(ws_t[:, :, :], ps[:, 2, :].rearrange("p (g f) -> p g f", g=GG), ACT.Copy).then_inc(wsT_ready, 1)
            project(0, first["out_ab"], 0)
            heads_T(0)
            attention(0)
            cat_T(0)
            for u in range(first["out_ab"], first["ffn"]):
                split_hi(act, u + SPLITS)
            act.wait_ge(router_loaded, 16)
            act.activation(router_hi[:, :, :], router[:, :, :], ACT.Copy).then_inc(router_hi_ready, 1)
            norm(1)
            act.preload_act_table(ACT.Silu)
            ffn()
            norm(2)
            project(first["in_cd"], first["conv"], 1)
            for z in range(3):
                for c in range(2):
                    split_hi(act, first["conv"] + 2 * z + c + SPLITS)
                act.wait_ge(unit_used, first["conv"] + 2 * z + 2)
                if z != 1:
                    act.activation(conv_z[:, :, :] if z == 0 else conv_b[:, :, :],
                                   ps[:, 4 + z, :].rearrange("p (c f) -> p c f", c=2), ACT.Copy).then_inc(cv_copied, 1)
            heads_T(1)
            attention(1)
            cat_T(1)
            for u in range(first["out_cd"], first["moe"]):
                split_hi(act, u + SPLITS)
            norm(3)
            act.wait_ge(xs_act, 8)
            act.wait_ge(xs_dve, 8)
            act.activation(xs_hi[:, :, :], xs[:, :, :], ACT.Copy).then_inc(xs_hi_ready, 1)
            act.preload_act_table(ACT.Exp)
            act.wait_ge(diff_ready, 1)
            act.activation(rt[:, T_EXP:T_EXP + 2], rt[:, T_DIFF:T_DIFF + 2], ACT.Exp).then_inc(exp_ready, 1)
            act.preload_act_table(ACT.Silu)

            def gathered(j1):
                for k in range(KD):
                    if k % 4 == 0:
                        act.wait_ge(gather_done, 2 * j1 + (k // 4 + 1))
                    g = gain_rows[3] + k
                    ins = act.activation(xg_hi[:, k, :], ps[:, 1 if k < 4 else 3, (k % 4) * P:(k % 4 + 1) * P], ACT.Copy,
                                         scale=colpar[:, g:g + 1])
                    if k % 4 == 3:
                        ins.then_inc(xg_hi_ready, 1)

            def turned_h(j, i):
                act.wait_ge(hT_done, SLABS * j + (i + 1))
                act.activation(mh_hi[:, :, :], ps[:, 4, :].rearrange("p (c f) -> p c f", c=4), ACT.Copy).then_inc(hT_hi, 1)

            def y_out(j):
                act.wait_ge(unit_used, j * JOB_UNITS + U_MOE)
                for half in range(2):
                    act.activation(y_hi[:, half * 512:(half + 1) * 512], bank(6 + half), ACT.Copy,
                                   scale=rt[:, T_GSLOT:T_GSLOT + 1]).then_inc(y_act, 1)

            gathered(0)
            act.wait_ge(y_zeroed, 1)
            act.wait_ge(meta_ready, 1)
            jobs = act.value_load(meta[0:1, 0:1], min_val=NE, max_val=JOBS_MAX)
            with act.Fori(0, jobs) as j:
                for w in range(SPLITS):
                    moe_split_hi(act, j, w)
                y_out(j)
                for v, (kind, i) in enumerate(job_steps):
                    for w in range(4 * v + SPLITS, min(4 * v + 4 + SPLITS, JOB_UNITS)):
                        moe_split_hi(act, j, w)
                    if kind == "g":
                        act.wait_ge(unit_used, j * JOB_UNITS + (U_MOE + 4 * v + 4))
                        if i >= 2:
                            act.wait_ge(h_ready, SLABS * j + (i - 1))
                        act.activation(msg[:, i % 2, :], bank(i % 2), ACT.Silu).then_inc(silu_ready, 1)
                        if i >= 1:
                            turned_h(j, i - 1)
                        if i == 2:
                            act.wait_ge(pickT_done, j + 1)
                            act.activation(pick_t[:, :, :], ps[:, 5, 0:TT * P].rearrange("p (t f) -> p t f", t=TT), ACT.Copy)
                            act.activation(rt[:, T_GSLOT:T_GSLOT + 1], ps[:, 5, TT * P:TT * P + 1],
                                           ACT.Copy).then_inc(pickT_ready, 1)
                    if kind == "d" and i == SLABS - 2:
                        turned_h(j, SLABS - 1)
                        gathered(j + 1)
            y_out(jobs)

        @block.vector
        def _(dve):
            chain = [0]

            def link(ins):
                chain[0] += 1
                ins.then_inc(dve_chain, 1)
                dve.wait_ge(dve_chain, chain[0])

            def norm(n):
                if n == 0:
                    dve.wait_ge(x_loaded, 16)
                else:
                    dve.wait_ge(res_added, n)
                link(dve.tensor_tensor_reduce(xs[:, 1, :], xres[:, 1, :], xres[:, 1, :], 1.0, 0.0, ALU.mult, ALU.add,
                                              small[:, SS + 1:SS + 2]))
                dve.wait_ge(sq_act, n + 1)
                dve.tensor_scalar(small[:, MS:MS + 2], small[:, SS:SS + 2], 1.0 / D, EPS, ALU.mult,
                                  ALU.add).then_inc(ms_ready, 1)
                dve.wait_ge(std_ready, n + 1)
                dve.reciprocal(small[:, RS:RS + 2], small[:, SD:SD + 2]).then_inc(rstd_ready, 1)
                dve.wait_ge(rstd_ready, n + 1)
                for half in range(2):
                    cs = slice(half * 512, half * 512 + 512)
                    dve.tensor_scalar(xs[:, 1, cs], xres[:, 1, cs], small[:, RS + 1:RS + 2], None,
                                      ALU.mult).then_inc(xs_dve, 1)
                if n == 0:
                    dve.wait_ge(setup_pe, 1)
                    dve.tensor_copy(colpar[:, 0:R_ROWS], ps[:, 0, 0:R_ROWS]).then_inc(col_ready, 1)
                    for u in range(SPLITS):
                        split_lo(dve, u)
                    dve.wait_ge(col_ready, 1)
                for q in range(4):
                    dve.wait_ge(xt_hi, 4 * n + q + 1)
                    for kk in range(2):
                        k = 2 * q + kk
                        g = gain_rows[n] + k
                        ins = dve.scalar_tensor_tensor(
                            out=act_lo[:, k, :], in0=ps[:, 4 + q, kk * SEQ:(kk + 1) * SEQ], scalar=colpar[:, g:g + 1],
                            in1=act_hi[:, k, :].bitcast(F32), op0=ALU.mult, op1=ALU.subtract)
                    ins.then_inc(xt_lo, 1)
                if n == 0:
                    dve.wait_ge(setup_pe, 2)
                    for c in (B_DQ, B_MQ):
                        dve.tensor_scalar(rowpar[:, c:c + HD], ps[:, 3, c:c + HD], QSCALE, None, ALU.mult)
                    dve.tensor_copy(rowpar[:, B_DK:B_DK + HD], ps[:, 3, B_DK:B_DK + HD])
                    dve.tensor_copy(rowpar[:, B_MK:512], ps[:, 3, B_MK:512]).then_inc(row_ready, 1)

            def group_sums(src, heads, dst):
                sq = tmp[:, 0, 0:heads * HD]
                link(dve.tensor_tensor(sq, src, src, ALU.mult))
                link(dve.tensor_reduce(dst, sq.rearrange("p (h d) -> p h d", d=HD), AX.X, ALU.add))

            roped = [None]

            def rope_next():
                if roped[0] is not None and roped[0] < ROPE_PARTS:
                    rope_part(dve, link, tmp[:, 0, :], 0, roped[0], q_roped)
                    roped[0] += 1

            def project(u0, u1, layer):
                u, c = u0, 0
                while u < u1:
                    t = units[u][0]
                    ncol = tiles[t][2]
                    b = (c % 2) * 2
                    while u < u1 and units[u][0] == t:
                        split_lo(dve, u + SPLITS)
                        u += 1
                        rope_next()
                    dve.wait_ge(unit_used, u)
                    m = col_tiles[layer][c]
                    if m != "g":
                        dst = pqk[:, 1, m * 512:m * 512 + ncol] if m < 3 else pv[:, 1, (m - 3) * 512:(m - 3) * 512 + ncol]
                        dve.tensor_copy(dst, bank(b + 1, ncol)).then_inc(proj_dve, 1)
                        dve.wait_ge(proj_dve, read_dve[layer][c])
                    dve.wait_ge(proj_act, read_act[layer][c])
                    if m == "g":
                        for t_ in range(TT):
                            group_sums(uv[:, t_, GW:2 * GW], GG, small[:, HSS + t_ * GG:HSS + (t_ + 1) * GG])
                        dve.tensor_scalar(small[:, HMS:HMS + 8], small[:, HSS:HSS + 8], 1.0 / HD, EPS,
                                          ALU.mult, ALU.add).then_inc(gv_ms, 1)
                    if m in (1, 2):
                        for t_ in range(TT):
                            for h0 in (0, 6):
                                c0 = (m - 1) * QW + h0 * HD
                                group_sums(pqk[:, t_, c0:c0 + 6 * HD], 6, head_sums(HSS, m - 1, t_)[:, h0:h0 + 6])
                    if m == 2:
                        dve.tensor_scalar(small[:, HMS + 8:HMS + HN], small[:, HSS + 8:HSS + HN], 1.0 / HD, EPS,
                                          ALU.mult, ALU.add).then_inc(head_ms, 1)
                        dve.wait_ge(head_std, layer + 1)
                        dve.reciprocal(small[:, HRS + 8:HRS + HN], small[:, HSD + 8:HSD + HN]).then_inc(head_rstd, 1)
                        dve.wait_ge(head_rstd, layer + 1)
                        dve.wait_ge(rope_ready, layer + 1)
                        roped[0] = 0
                    if m == 3 and layer == 0:
                        dve.wait_ge(gv_std, 1)
                        link(dve.reciprocal(small[:, HRS:HRS + 8], small[:, HSD:HSD + 8]))
                        for t_ in range(TT):
                            v = uv[:, t_, GW:2 * GW].rearrange("p (g d) -> p g d", g=GG)
                            rs = small[:, HRS + t_ * GG:HRS + (t_ + 1) * GG]
                            link(dve.tensor_tensor(v, v, rs.unsqueeze(2).broadcast_to([P, GG, HD]), ALU.mult))
                            ins = dve.tensor_tensor(uv[:, t_, GW:2 * GW], uv[:, t_, GW:2 * GW],
                                                    rowpar[:, B_GV:B_GV + GW], ALU.mult)
                        ins.then_inc(gv_ready, 1)
                    c += 1

            def heads_T(layer):
                for r in (1, 3, 5):
                    dve.wait_ge(qkT_done, 6 * layer + r + 1)
                    dst = qT if r < 3 else kT
                    dve.tensor_copy(dst[:, 2 * (r % 3):2 * (r % 3) + 2, :],
                                    ps[:, (4 + r) % 8, :].rearrange("p (b f) -> p b f", b=2)).then_inc(qkT_dve, 1)

            def attention(layer):
                o0 = 8 * layer
                dve.wait_ge(masks_loaded, 16)
                for n in range(10):
                    if n < 8:
                        tt, hs = heads_of[layer][n]
                        keys = P * (tt + 1)
                        dve.wait_ge(s_done, o0 + n + 1)
                        if n >= 2:
                            dve.wait_ge(pT_done, o0 + n - 1)
                        if layer == 0:
                            m0 = (M_DIL0, M_DIL1)[tt]
                            link(dve.tensor_tensor_reduce(
                                probs[:, n % 2, 0:3 * keys].rearrange("p (s k) -> p s k", s=3), scores_psum_all(n, keys),
                                msk[:, m0:m0 + 3 * keys].rearrange("p (s k) -> p s k", s=3), 1.0, NEG, ALU.add, ALU.max,
                                small[:, MX + 3 * n:MX + 3 * n + 1]))
                            dve.tensor_scalar(small[:, NM + 3 * n:NM + 3 * n + 1], small[:, MX + 3 * n:MX + 3 * n + 1],
                                              -1.0, None, ALU.mult).then_inc(max_ready, 1)
                        else:
                            m0 = M_CAUSAL + P - tt * P
                            for seg in range(3):
                                ins = dve.tensor_tensor_reduce(
                                    probs[:, n % 2, seg * keys:(seg + 1) * keys], scores_psum(n, seg, keys),
                                    msk[:, m0:m0 + keys], 1.0, NEG, ALU.add, ALU.max,
                                    small[:, MX + 3 * n + seg:MX + 3 * n + seg + 1])
                            link(ins)
                            dve.tensor_scalar(small[:, NM + 3 * n:NM + 3 * n + 3], small[:, MX + 3 * n:MX + 3 * n + 3],
                                              -1.0, None, ALU.mult).then_inc(max_ready, 1)
                    if n == 1 and layer == 0:
                        dve.wait_ge(gy_done, 1)
                        y = ps[:, 6, :].rearrange("p (t g d) -> p t g d", t=TT, g=GG)
                        for g in range(GG):
                            ins = dve.scalar_tensor_tensor(
                                out=cat_ab[:, :, g * HD:(g + 1) * HD], in0=y[:, :, g, :],
                                scalar=colpar[:, R_BS + g:R_BS + g + 1], in1=uv[:, :, g * HD:(g + 1) * HD],
                                op0=ALU.add, op1=ALU.mult)
                        ins.then_inc(gcat_ready, 1)
                    if n >= 2:
                        m = n - 2
                        tt, hs = heads_of[layer][m]
                        ns = 3 if layer else 1
                        c = 3 * m
                        dve.wait_ge(p_ready, o0 + m + 1)
                        link(dve.reciprocal(small[:, RL + c:RL + c + ns], small[:, LS + c:LS + c + ns]))
                        dve.wait_ge(o_done, o0 + m + 1)
                        if layer == 0:
                            d0 = GW + (m % 4) * HD
                            dve.tensor_scalar(cat_ab[:, tt, d0:d0 + HD], ps[:, 7 - m % 2, 0:HD], small[:, RL + c:RL + c + 1],
                                              None, ALU.mult).then_inc(o_ready, 1)
                        else:
                            d0 = (hs[0] - hs[0] % 2) * HD
                            dst = cat_c[tt][:, d0:d0 + 6 * HD].rearrange("p (s d) -> p s d", s=3)
                            dve.tensor_tensor(dst[:, :, (hs[0] % 2) * HD:(hs[0] % 2 + 1) * HD],
                                              ps[:, 7 - m % 2, 0:3 * HD].rearrange("p (s d) -> p s d", s=3),
                                              small[:, RL + c:RL + c + 3].unsqueeze(2).broadcast_to([P, 3, HD]),
                                              ALU.mult).then_inc(o_ready, 1)

            def cat_T(layer):
                for r in range(2 + layer):
                    dve.wait_ge(ct_hi, 2 * layer + r + 1)
                    dve.tensor_tensor(act_lo[:, 2 * r:2 * r + 2, :], ps[:, r, :].rearrange("p (b f) -> p b f", b=2),
                                      act_hi[:, 2 * r:2 * r + 2, :].bitcast(F32), ALU.subtract).then_inc(ct_lo, 1)
                if layer == 1:
                    dve.wait_ge(ct_hi, 6)
                    dve.tensor_tensor(act_lo[:, 6:8, :], conv_y[:, :, :], act_hi[:, 6:8, :].bitcast(F32),
                                      ALU.subtract).then_inc(ct_lo, 1)

            def residual(u_end):
                dve.wait_ge(unit_used, u_end)
                for t in range(TT):
                    for half in range(2):
                        v = xres[:, t, half * 512:(half + 1) * 512]
                        ins = dve.tensor_tensor(v, v, bank(4 + 2 * t + half), ALU.add)
                ins.then_inc(res_added, 1)

            def ffn():
                u = first["ffn"]
                for s in range(len(widths) + 1):
                    if s < len(widths):
                        for bb in range(widths[s] // P):
                            b = block_first[s] + bb
                            split_lo(dve, u + SPLITS)
                            split_lo(dve, u + 1 + SPLITS)
                            u += 2
                            dve.wait_ge(fsg_ready, b + 1)
                            dve.tensor_tensor(fh[:, b % 2, :], fsg[:, b % 2, :], ps[:, b % 4, SEQ:2 * SEQ],
                                              ALU.mult).then_inc(fh_ready, 1)
                            dve.wait_ge(fh_hi_ready, b + 1)
                            dve.tensor_tensor(fh_lo[:, s % 2, bb, :], fh[:, b % 2, :], fh_hi[:, s % 2, bb, :].bitcast(F32),
                                              ALU.subtract).then_inc(fh_lo_ready, 1)
                    if s >= 1:
                        for c in range(widths[s - 1] // P):
                            split_lo(dve, u + SPLITS)
                            u += 1

            norm(0)
            project(0, first["out_ab"], 0)
            heads_T(0)
            attention(0)
            cat_T(0)
            for u in range(first["out_ab"], first["ffn"]):
                split_lo(dve, u + SPLITS)
            residual(first["ffn"])
            norm(1)
            dve.wait_ge(router_hi_ready, 1)
            dve.tensor_tensor(router_lo[:, :, :], router[:, :, :], router_hi[:, :, :].bitcast(F32),
                              ALU.subtract).then_inc(router_lo_ready, 1)
            ffn()
            residual(first["in_cd"])
            norm(2)
            project(first["in_cd"], first["conv"], 1)
            for z in range(3):
                for c in range(2):
                    split_lo(dve, first["conv"] + 2 * z + c + SPLITS)
                    rope_next()
                if z == 1:
                    dve.wait_ge(unit_used, first["conv"] + 4)
                    dve.wait_ge(cv_copied, 1)
                    dve.tensor_tensor(conv_z[:, :, :], conv_z[:, :, :], ps[:, 5, :].rearrange("p (c f) -> p c f", c=2),
                                      ALU.mult).then_inc(cv_z, 1)
            heads_T(1)
            attention(1)
            cat_T(1)
            for u in range(first["out_cd"], first["moe"]):
                split_lo(dve, u + SPLITS)
            residual(first["moe"])
            norm(3)

            def r(c, n=1):
                return rt[:, c:c + n]

            def r2(c):
                return rt[:, c:c + TT * NE]

            dve.wait_ge(xs_hi_ready, 1)
            dve.wait_ge(xs_act, 8)
            dve.wait_ge(xs_dve, 8)
            dve.tensor_tensor(xs_lo[:, :, :], xs[:, :, :], xs_hi[:, :, :].bitcast(F32), ALU.subtract).then_inc(xs_lo_ready, 1)
            dve.wait_ge(zeroed, 1)
            dve.wait_ge(lg_done, 1)
            link(dve.tensor_copy(r2(T_LG), ps[:, 0, 0:TT * NE]))
            for t in range(TT):
                ins = dve.max(r(T_MX + t * NE, NE), r(T_LG + t * NE, NE))
            link(ins)
            mx = r2(T_MX).rearrange("p (t e) -> p t e", t=TT)
            dve.tensor_tensor(r(T_DIFF, TT).unsqueeze(2), mx[:, :, 1:2], mx[:, :, 0:1], ALU.subtract).then_inc(diff_ready, 1)
            for t in range(TT):
                lg = r(T_LG + t * NE, NE)
                other = lg.unsqueeze(1).broadcast_to([P, NE, NE])
                own = lg.unsqueeze(2).broadcast_to([P, NE, NE])
                c1 = r(T_CMP + t * 64, 64).rearrange("p (e f) -> p e f", e=NE)
                c2 = r(T_CMP2 + t * 64, 64).rearrange("p (e f) -> p e f", e=NE)
                dve.tensor_tensor(c1, other, own, ALU.is_gt)
                link(dve.tensor_tensor(c2, other, own, ALU.is_equal))
                link(dve.tensor_tensor(c2, c2, cst[:, C_LT:C_LT + 64].rearrange("p (e f) -> p e f", e=NE), ALU.mult))
                link(dve.tensor_tensor(c1, c1, c2, ALU.add))
                ins = dve.tensor_reduce(r(T_RANK + t * NE, NE), c1, AX.X, ALU.add)
            link(ins)
            dve.tensor_scalar(r2(T_SEL), r2(T_RANK), 1.5, None, ALU.is_lt).then_inc(sel_ready, 1)
            dve.wait_ge(sel_ready, 1)
            link(dve.tensor_scalar(r2(T_TMP), r2(T_RANK), 0.5, None, ALU.is_lt))
            dve.wait_ge(exp_ready, 1)
            link(dve.tensor_scalar(r(T_DEN, TT), r(T_EXP, TT), 1.0, None, ALU.add))
            link(dve.reciprocal(r(T_G1, TT), r(T_DEN, TT)))
            link(dve.tensor_tensor(r(T_G2, TT), r(T_G1, TT), r(T_EXP, TT), ALU.mult))
            link(dve.tensor_tensor(r2(T_Q), r2(T_SEL), r2(T_TMP), ALU.subtract))
            for t in range(TT):
                ins = dve.tensor_scalar(r(T_Q + t * NE, NE), r(T_Q + t * NE, NE), r(T_G2 + t), None, ALU.mult)
            link(ins)
            for t in range(TT):
                ins = dve.scalar_tensor_tensor(out=r(T_GATE + t * NE, NE), in0=r(T_TMP + t * NE, NE), scalar=r(T_G1 + t),
                                               in1=r(T_Q + t * NE, NE), op0=ALU.mult, op1=ALU.add)
            link(ins)
            dve.wait_ge(cnt_done, 1)
            link(dve.tensor_scalar(r(T_POS, TT * NE), ps[:, 1, 0:TT * NE], 1.0, None, ALU.add))
            dve.tensor_scalar(r(T_OVER, NE), ps[:, 1, TT * NE:TT * NE + NE], P + 0.5, None, ALU.is_gt)
            link(dve.tensor_tensor(r2(T_POS), r2(T_POS), r2(T_SEL), ALU.mult))
            for t in range(TT):
                dve.tensor_scalar(r(T_JP + t * JCOLS, NE), r(T_POS + t * NE, NE), -1.0, None, ALU.add)
                ins = dve.tensor_copy(r(T_JG + t * JCOLS, NE), r(T_GATE + t * NE, NE))
            link(ins)
            def choose(jn):
                for t in range(TT):
                    jp = rt[:, bass.ds(jn + (T_JP + t * JCOLS), 1)]
                    jg = rt[:, bass.ds(jn + (T_JG + t * JCOLS), 1)]
                    dve.tensor_copy(rt[:, T_GTOK + t:T_GTOK + t + 1], jg)
                    ins = dve.tensor_scalar(pick[:, t, :], cst[:, C_IOTA:C_IOTA + P], jp, None, ALU.is_equal)
                ins.then_inc(pick_ready, 1)

            def gathered(j1):
                for k in range(KD):
                    if k % 4 == 0:
                        dve.wait_ge(xg_hi_ready, 2 * j1 + (k // 4 + 1))
                    g = gain_rows[3] + k
                    ins = dve.scalar_tensor_tensor(
                        out=xg_lo[:, k, :], in0=ps[:, 1 if k < 4 else 3, (k % 4) * P:(k % 4 + 1) * P],
                        scalar=colpar[:, g:g + 1], in1=xg_hi[:, k, :].bitcast(F32), op0=ALU.mult, op1=ALU.subtract)
                    if k % 4 == 3:
                        ins.then_inc(xg_lo_ready, 1)

            def turned_h(j, i):
                dve.wait_ge(hT_hi, SLABS * j + (i + 1))
                dve.tensor_tensor(mh_lo[:, :, :], ps[:, 4, :].rearrange("p (c f) -> p c f", c=4),
                                  mh_hi[:, :, :].bitcast(F32), ALU.subtract).then_inc(hT_lo, 1)

            def y_out(j):
                for half in range(2):
                    cs = slice(half * 512, half * 512 + 512)
                    dve.wait_ge(y_act, 2 * j + (half + 1))
                    ins = dve.scalar_tensor_tensor(out=y_lo[:, cs], in0=bank(6 + half), scalar=rt[:, T_GSLOT:T_GSLOT + 1],
                                                   in1=y_hi[:, cs].bitcast(F32), op0=ALU.mult, op1=ALU.subtract)
                ins.then_inc(y_dve, 1)

            def add_out(j):
                dve.wait_ge(comb_done, j + 1)
                dve.wait_ge(lo_ready, j * JOB_UNITS + U_MOE)
                for n, b in enumerate((5, 4, 3, 1)):
                    t, half = divmod(n, 2)
                    v = xres[:, t, half * 512:(half + 1) * 512]
                    ins = dve.tensor_tensor(v, v, bank(b), ALU.add)
                ins.then_inc(comb_added, 1)

            choose(0)
            c1 = r(T_CMP, 64).rearrange("p (e f) -> p e f", e=NE)
            link(dve.tensor_tensor(c1, r(T_OVER, NE).unsqueeze(1).broadcast_to([P, NE, NE]),
                                   cst[:, C_LT:C_LT + 64].rearrange("p (e f) -> p e f", e=NE), ALU.mult))
            link(dve.tensor_reduce(r(T_OIDX, NE), c1, AX.X, ALU.add))
            link(dve.scalar_tensor_tensor(out=r2(T_Q), in0=r2(T_SEL), scalar=-float(P), in1=r2(T_POS), op0=ALU.mult, op1=ALU.add))
            for k in range(JOBS_MAX - NE):
                ins = dve.scalar_tensor_tensor(out=r(T_W + k * NE, NE), in0=r(T_OIDX, NE), scalar=float(k), in1=r(T_OVER, NE),
                                               op0=ALU.is_equal, op1=ALU.mult)
            link(ins)
            for k in range(JOBS_MAX - NE):
                w = r(T_W + k * NE, NE)
                for t in range(TT):
                    c = t * JCOLS + NE + k
                    link(dve.tensor_tensor_reduce(r(T_JUNK, NE), r(T_Q + t * NE, NE), w, 1.0, -1.0, ALU.mult, ALU.add, r(T_JP + c)))
                    link(dve.tensor_tensor_reduce(r(T_JUNK, NE), r(T_GATE + t * NE, NE), w, 1.0, 0.0, ALU.mult, ALU.add, r(T_JG + c)))
                link(dve.tensor_tensor_reduce(r(T_JUNK, NE), cst[:, C_IOTA:C_IOTA + NE], w, 1.0, 0.0, ALU.mult, ALU.add,
                                              r(T_F + 2 + k)))
            link(dve.tensor_reduce(r(T_F), r(T_OVER, NE), AX.X, ALU.add))
            link(dve.tensor_scalar(r(T_F), r(T_F), float(NE), None, ALU.add))
            link(dve.memset(r(T_F + 1), float(NE - 1)))
            dve.tensor_copy(meta[:, 0:5], r(T_F, 5)).then_inc(meta_ready, 1)
            gathered(0)
            dve.wait_ge(y_zeroed, 1)
            dve.wait_ge(meta_ready, 1)
            jobs = dve.value_load(meta[0:1, 0:1], min_val=NE, max_val=JOBS_MAX)
            with dve.Fori(0, jobs) as j:
                for w in range(SPLITS):
                    moe_split_lo(dve, j, w)
                y_out(j)
                for v, (kind, i) in enumerate(job_steps):
                    for w in range(4 * v + SPLITS, min(4 * v + 4 + SPLITS, JOB_UNITS)):
                        moe_split_lo(dve, j, w)
                    if kind == "g" and i == 0:
                        add_out(j)
                    if kind == "g" and i >= 1:
                        turned_h(j, i - 1)
                    if kind == "g" and i == 2:
                        dve.wait_ge(pickT_done, j + 1)
                        dve.wait_ge(gather_done, 2 * j + 2)
                        choose(j + 1)
                    if kind == "u":
                        dve.wait_ge(silu_ready, SLABS * j + (i + 1))
                        dve.wait_ge(unit_used, j * JOB_UNITS + (U_MOE + 4 * v + 4))
                        if i >= 2:
                            dve.wait_ge(hT_done, SLABS * j + (i - 1))
                        dve.tensor_tensor(mh[:, i % 2, :], msg[:, i % 2, :], bank(2 + i % 2), ALU.mult).then_inc(h_ready, 1)
                    if kind == "d" and i == SLABS - 2:
                        turned_h(j, SLABS - 1)
                        gathered(j + 1)
            y_out(jobs)
            add_out(jobs)


_INS = ["x", "norm_mix", "norm_ffn", "w_in_ab", "gmlp_v_gain", "gmlp_ws", "gmlp_bs", "dil_q_gain", "dil_k_gain",
        "w_out_ab", "ffn_w_gate", "ffn_w_up", "ffn_w_down", "w_in_cd", "moba_q_gain", "moba_k_gain", "conv_w",
        "w_out_cd", "router_w", "moe_w_gate", "moe_w_up", "moe_w_down"]


def kernel(**inputs):
    import concourse.bacc as bacc
    from concourse.bass_utils import run_bass_kernel_spmd

    nc = bacc.Bacc("TRN2", target_bir_lowering=False, num_devices=1)
    arrays, args = {}, []
    for name in _INS:
        a = np.ascontiguousarray(inputs[name])
        arrays[f"in_{name}"] = a
        args.append(nc.dram_tensor(f"in_{name}", a.shape, mybir.dt.from_np(a.dtype), kind="ExternalInput").ap())
    for name, a in zip(("const_f32", "const_mask"), constant_tables()):
        arrays[name] = a
        args.append(nc.dram_tensor(name, a.shape, mybir.dt.from_np(a.dtype), kind="ExternalInput").ap())
    args.append(nc.dram_tensor("out", (1, SEQ, D), F32, kind="ExternalOutput").ap())
    decoder_trunk(nc, *args)
    r = run_bass_kernel_spmd(nc, [arrays], core_ids=[0])
    return r.results[0]["out"]
```

```python
from contextlib import ExitStack

import numpy as np

import concourse.bass as bass
from concourse import mybir

F32 = mybir.dt.float32
F32R = mybir.dt.float32r
BF16 = mybir.dt.bfloat16
I32 = mybir.dt.int32
ACT = mybir.ActivationFunctionType
ALU = mybir.AluOpType
AX = mybir.AxisListType

P = 128
SEQ, D = 256, 1024
TT = SEQ // P
KD = D // P
HD = 64
HH = HD // 2
GW = 256
GG = 4
HEADS = 12
QW = HEADS * HD
CW = 256
FF = 2816
FE = 3584
NE = 8
EPS = 1e-6
QSCALE = HD ** -0.5
NEG = -1e30

RING = 7
TILE = 4096
UNIT = 1024
SPLITS = 4
SLAB = 512
SLABS = FE // SLAB
JOB_TILES = 3 * SLABS
JOB_UNITS = JOB_TILES * TILE // UNIT
JOBS_MAX = NE + 3
JCOLS = JOBS_MAX + 1

OUT_CD_ORDER = (6, 7, 4, 5, 0, 1, 2, 3)

C_ID, C_IOTA, C_UP, C_ONE = 0, 128, 256, 384
C_COS, C_SIN, C_LT = 512, 640, 768
C_COLS = C_LT + 64
M_DIL0, M_DIL1, M_CAUSAL = 0, 384, 1152
M_COLS = M_CAUSAL + 256

R_MIX, R_FFN, R_BS, R_CONV = 0, 16, 32, 36
R_ROWS = R_CONV + 6
B_DQ, B_DK, B_MQ, B_MK, B_GV = 0, 64, 128, 192, 256


def constant_tables():
    c = np.zeros((P, C_COLS), np.float32)
    p = np.arange(P)
    c[:, C_ID:C_ID + P] = np.eye(P)
    c[:, C_IOTA:C_IOTA + P] = np.arange(P)[None, :]
    c[:, C_UP:C_UP + P] = p[:, None] < p[None, :]
    c[:, C_ONE:C_ONE + P] = 1.0
    inv = (1.0 / (np.float32(10000.0) ** (np.arange(0, HD, 2, dtype=np.float32) / HD))).astype(np.float32)
    ang = np.arange(SEQ, dtype=np.float32)[:, None] * inv[None, :]
    cos, sin = np.cos(ang).astype(np.float32), np.sin(ang).astype(np.float32)
    for t in range(TT):
        rows = slice(t * P, t * P + P)
        c[:, C_COS + t * HD:C_COS + (t + 1) * HD] = np.concatenate([cos[rows], cos[rows]], 1)
        c[:, C_SIN + t * HD:C_SIN + (t + 1) * HD] = np.concatenate([-sin[rows], sin[rows]], 1)
    e = np.arange(NE)
    c[:, C_LT:C_LT + 64] = (e[None, :] < e[:, None]).reshape(1, 64)

    m = np.zeros((P, M_COLS), np.float32)
    for t, base in ((0, M_DIL0), (1, M_DIL1)):
        keys = P * (t + 1)
        q = (t * P + p)[:, None]
        k = np.arange(keys)[None, :]
        for g, (window, dil) in enumerate(((128, 1), (512, 4), (2048, 16))):
            seen = (k <= q) & ((q - k) % dil == 0) & ((q - k) // dil <= window // dil)
            m[:, base + g * keys:base + (g + 1) * keys] = np.where(seen, 0.0, NEG)
    m[:, M_CAUSAL + P:M_CAUSAL + 2 * P] = np.where(p[None, :] <= p[:, None], 0.0, NEG)
    return c, m


def weight_stream(w_in_ab, w_out_ab, ffn_g, ffn_u, ffn_d, w_in_cd, w_out_cd):
    tiles, units = [], []

    def tile(w, row0, nrow, col0, ncol):
        tiles.append((w[row0:row0 + nrow * P, col0:col0 + ncol].rearrange("(k p) f -> p k f", p=P), nrow, ncol))
        return len(tiles) - 1

    def by_rows(t):
        _, nrow, ncol = tiles[t]
        n = UNIT // ncol
        return [(t, r, n, 0, ncol) for r in range(0, nrow, n)]

    def by_columns(t):
        _, nrow, ncol = tiles[t]
        return [(t, 0, nrow, c, P) for c in range(0, ncol, P)]

    first = {"in_ab": 0}
    for c in (2 * GW, 2 * GW + SLAB, 2 * GW + 2 * SLAB, 0, 2 * GW + 3 * SLAB, 2 * GW + 4 * SLAB):
        units += by_rows(tile(w_in_ab, 0, KD, c, min(SLAB, 2 * GW + 3 * QW - c)))
    first["out_ab"] = len(units)
    units += by_rows(tile(w_out_ab, 0, 4, 0, D))
    first["ffn"] = len(units)
    widths = [min(SLAB, FF - c) for c in range(0, FF, SLAB)]
    for s in range(len(widths) + 1):
        if s < len(widths):
            tg = tile(ffn_g, 0, KD, s * SLAB, widths[s])
            tu = tile(ffn_u, 0, KD, s * SLAB, widths[s])
            for g, u in zip(by_columns(tg), by_columns(tu)):
                units += [g, u]
        if s >= 1:
            units += by_rows(tile(ffn_d, (s - 1) * SLAB, widths[s - 1] // P, 0, D))
    first["in_cd"] = len(units)
    for c in range(0, 3 * QW, SLAB):
        units += by_rows(tile(w_in_cd, 0, KD, c, min(SLAB, 3 * QW - c)))
    first["conv"] = len(units)
    for c in (3 * QW + CW, 3 * QW + 2 * CW, 3 * QW):
        units += by_columns(tile(w_in_cd, 0, KD, c, CW))
    first["out_cd"] = len(units)
    last = by_rows(tile(w_out_cd, 4 * P, 4, 0, D))
    units += last[2:] + last[:2] + by_rows(tile(w_out_cd, 0, 4, 0, D))
    first["moe"] = len(units)
    return tiles, units, first, widths


def decoder_trunk(nc, x, norm_mix, norm_ffn, w_in_ab, gmlp_v_gain, gmlp_ws, gmlp_bs, dil_q_gain, dil_k_gain,
                  w_out_ab, ffn_w_gate, ffn_w_up, ffn_w_down, w_in_cd, moba_q_gain, moba_k_gain, conv_w,
                  w_out_cd, router_w, moe_w_gate, moe_w_up, moe_w_down, const_f32, const_mask, out):
    tiles, units, first, widths = weight_stream(w_in_ab[0], w_out_ab[0], ffn_w_gate[0], ffn_w_up[0],
                                                ffn_w_down[0], w_in_cd[0], w_out_cd[0])
    U_MOE, T_MOE = len(units), len(tiles)
    assert U_MOE % SPLITS == 0 and JOB_UNITS % SPLITS == 0 and T_MOE % RING == 0 and JOB_TILES % RING == 0
    tile_last = {}
    for u, un in enumerate(units):
        tile_last[un[0]] = u

    with ExitStack() as ctx:
        base = (nc.sbuf_base + 31) // 32 * 32
        place = [base]

        def at(name, shape, dt, offset):
            return nc.alloc_sbuf_tensor_at(name, [P, *shape], dt, offset=offset)

        def keep(name, shape, dt=F32):
            size = int(np.prod(shape)) * (2 if dt == BF16 else 4)
            t = at(name, shape, dt, place[0])
            place[0] += (size + 31) // 32 * 32
            return t

        raw = keep("raw_ring", [RING, TILE])
        wh = keep("w_hi", [SPLITS, UNIT], F32R)
        wl = keep("w_lo", [SPLITS, UNIT], F32R)
        xres = keep("x_residual", [TT, D])
        cst = keep("const", [C_COLS])
        colpar = keep("col_params", [48])
        router = keep("router", [KD, NE])
        router_hl = keep("router_hi_lo", [KD, 2, NE], F32R)
        small = keep("small", [352])
        meta = keep("meta", [8], I32)
        xs_lo = at("x_scaled_lo", [TT, D], F32R, place[0])
        msk = keep("masks", [M_COLS], BF16)
        rope_t = keep("rope_tables", [4, TT, HD])
        rowpar = keep("row_params", [512])
        ws_t = keep("gmlp_wT", [GG, P])
        R0 = place[0]
        act_hi = at("act_hi", [KD, SEQ], F32R, R0)
        act_lo = at("act_lo", [KD, SEQ], F32R, R0 + 8192)
        R1 = R0 + 16384
        end = R1 + 25600
        assert end <= nc.sbuf_usable_end, (end, nc.sbuf_usable_end)
        par_rows = at("par_rows", [P], F32, R1 + 8192)
        row_src = at("row_src", [512], F32, R1 + 8192 + 512)
        ws_in = at("gmlp_ws_in", [GG, P], F32, R1 + 8192 + 512 + 2048)
        xs = at("x_scaled", [TT, D], F32, R1)
        pqk = at("p_qk", [TT, 2 * QW], F32, R1)
        pv = at("p_v", [TT, QW], F32, R1 + 12288)
        uv = at("p_uv", [TT, 2 * GW], F32, R1 + 18432)
        tmp = at("rope_tmp", [2, QW // 2], F32, R1 + 22528)
        qT = at("qT", [6, SEQ], F32, R0)
        kT = at("kT", [6, SEQ], F32, R0 + 6144)
        cat_ab = at("cat_ab", [TT, 512], F32, R0 + 12288)
        cat_c = [at("cat_c0", [QW], F32, R1 + 22528), at("cat_c1", [QW], F32, R1 + 19456)]
        probs = at("probs", [2, 768], F32, R1)
        probs_t = at("probs_T", [2, 768], F32, R1 + 6144)
        conv_z = at("conv_z", [2, SEQ], F32, R1 + 18432)
        conv_y = at("conv_y", [2, SEQ], F32, R0 + 12288)
        conv_b = at("conv_b", [2, SEQ], F32, R0 - 2048)
        fh_hi = at("ffn_h_hi", [2, 4, SEQ], F32R, R1)
        fh_lo = at("ffn_h_lo", [2, 4, SEQ], F32R, R1 + 8192)
        fsg = at("ffn_silu", [2, SEQ], F32, R1 + 16384)
        fh = at("ffn_h", [2, SEQ], F32, R1 + 18432)
        xg_hi = at("xg_hi", [KD, P], F32R, R0)
        xg_lo = at("xg_lo", [KD, P], F32R, R0 + 4096)
        msg = at("moe_silu", [2, SLAB], F32, R0 + 8192)
        mh = at("moe_h", [2, SLAB], F32, R0 + 12288)
        mh_hi = at("moe_hT_hi", [4, P], F32R, R1)
        mh_lo = at("moe_hT_lo", [4, P], F32R, R1 + 2048)
        y_hi = at("moe_y_hi", [D], F32R, R1 + 4096)
        xs_hi = at("x_scaled_hi", [TT, D], F32R, R1 + 8192)
        y_lo = at("moe_y_lo", [D], F32R, R1 + 16384)
        pick = at("pick", [TT, P], F32R, R1 + 20480)
        pick_t = at("pick_T", [TT, P], F32R, R1 + 21504)
        rt = at("routing", [520], F32, R1 + 22528)
        count_t = at("count_tables", [2, P], BF16, R1 + 24608)
        sel_b = at("selected", [TT, NE], BF16, R1 + 25120)

        ps = ctx.enter_context(nc.psum_tensor("psum", [P, 8, 512], F32))

        ident = cst[:, C_ID:C_ID + P]

        def sem(name):
            return ctx.enter_context(nc.semaphore(name))

        slot_loaded = [sem(f"slot_loaded{i}") for i in range(RING)]
        first_part_loaded = sem("first_part_loaded")
        x_loaded, const_loaded, par_loaded = sem("x_loaded"), sem("const_loaded"), sem("par_loaded")
        rows_loaded, ws_loaded, router_loaded = sem("rows_loaded"), sem("ws_loaded"), sem("router_loaded")
        hi_ready, lo_ready, unit_used = sem("hi_ready"), sem("lo_ready"), sem("unit_used")
        dve_chain, act_chain, pool_chain = sem("dve_chain"), sem("act_chain"), sem("pool_chain")
        setup_pe, ws_masked, wsT_ready = sem("setup_pe"), sem("ws_masked"), sem("wsT_ready")
        col_ready, row_ready, rope_ready = sem("col_ready"), sem("row_ready"), sem("rope_ready")
        sq_act, ms_ready, std_ready, rstd_ready = sem("sq_act"), sem("ms_ready"), sem("std_ready"), sem("rstd_ready")
        xs_act, xs_dve = sem("xs_act"), sem("xs_dve")
        xt_done, xt_hi, xt_lo = sem("xt_done"), sem("xt_hi"), sem("xt_lo")
        proj_act = sem("proj_act")
        sq_ready, sq_used = sem("squares_ready"), sem("squares_used")
        head_ms, head_std, head_rstd = sem("head_ms"), sem("head_std"), sem("head_rstd")
        q_roped, k_roped = sem("q_roped"), sem("k_roped")
        gv_ms, gv_std, gv_rstd, gv_ready = sem("gv_ms"), sem("gv_std"), sem("gv_rstd"), sem("gv_ready")
        router_hi_ready, router_lo_ready = sem("router_hi_ready"), sem("router_lo_ready")
        xs_hi_ready, xs_lo_ready, masks_loaded = sem("xs_hi_ready"), sem("xs_lo_ready"), sem("masks_loaded")
        qkT_done, qkT_act, qkT_dve = sem("qkT_done"), sem("qkT_act"), sem("qkT_dve")
        gy_done, gcat_ready = sem("gy_done"), sem("gcat_ready")
        s_done, max_ready, p_ready = sem("scores_done"), sem("max_ready"), sem("probs_ready")
        pT_done, pT_ready, o_done, o_ready = sem("probsT_done"), sem("probsT_ready"), sem("o_done"), sem("o_ready")
        ct_done, ct_hi, ct_lo = sem("catT_done"), sem("catT_hi"), sem("catT_lo")
        sum_done, res_added = sem("sum_done"), sem("residual_added")
        fsg_ready, fh_ready, fh_hi_ready, fh_lo_ready = (
            sem("ffn_silu_ready"), sem("ffn_h_ready"), sem("ffn_h_hi"), sem("ffn_h_lo"))
        cv_copied, cv_z, cv_ready = sem("conv_copied"), sem("conv_z_ready"), sem("conv_ready")
        lg_done, diff_ready, exp_ready, sel_ready = sem("logits_done"), sem("diff_ready"), sem("exp_ready"), sem("sel_ready")
        count_ready = sem("count_tables_ready")
        cnt_done, meta_ready = sem("counts_done"), sem("meta_ready")
        pick_ready, gather_done, xg_hi_ready, xg_lo_ready = (
            sem("pick_ready"), sem("gather_done"), sem("xg_hi_ready"), sem("xg_lo_ready"))
        silu_ready, h_ready = sem("silu_ready"), sem("h_ready")
        hT_done, hT_hi, hT_lo = sem("hT_done"), sem("hT_hi"), sem("hT_lo")
        y_zeroed, y_act, y_dve = sem("y_zeroed"), sem("y_act"), sem("y_dve")
        last_done, last_added = sem("last_done"), sem("last_added")
        comb_done, comb_added = sem("combine_done"), sem("combine_added")
        pickT_done, pickT_ready, zeroed = sem("pickT_done"), sem("pickT_ready"), sem("zeroed")
        out_stored = sem("out_stored")

        SS, MS, SD, RS = 0, 2, 4, 6
        HSS, HMS, HSD, HRS, HN = 16, 72, 128, 184, 56
        MX, NM, LS, RL = 240, 264, 288, 312

        def head_sums(at_, which, t):
            c = at_ + 8 + (which * TT + t) * HEADS
            return small[:, c:c + HEADS]

        T_SEL, T_RANK, T_GATE, T_LG, T_MX, T_DIFF, T_EXP, T_G1, T_G2, T_DEN = 0, 16, 32, 48, 64, 80, 82, 84, 86, 88
        T_TMP, T_POS, T_OVER, T_OIDX, T_W, T_Q, T_JP, T_JG = 96, 112, 136, 144, 152, 176, 192, 216
        T_F, T_CMP, T_CMP2 = 240, 256, 384
        T_GTOK, T_GSLOT = 512, 514

        def bank(b, cols=512):
            return ps[:, b, 0:cols]

        def raw_unit(u):
            t, r0, n, c0, w = units[u]
            _, nrow, ncol = tiles[t]
            full = raw[:, t % RING, 0:nrow * ncol].rearrange("p (k f) -> p k f", f=ncol)
            return full[:, r0:r0 + n, c0:c0 + w]

        def part(buf, u, w):
            return buf[:, u % SPLITS, :].rearrange("p (k f) -> p k f", f=w)

        def split_hi(act, u):
            if u >= U_MOE:
                return
            t, r0, n, _, w = units[u]
            if t == 0 and r0 + n <= tiles[0][1] // 2:
                act.wait_ge(first_part_loaded, 16)
            else:
                act.wait_ge(slot_loaded[t % RING], 16 * (t // RING + 1))
            if u >= SPLITS:
                act.wait_ge(unit_used, u - SPLITS + 1)
            act.activation(part(wh, u, w), raw_unit(u), ACT.Copy).then_inc(hi_ready, 1)

        def split_lo(dve, u):
            if u >= U_MOE:
                return
            w = units[u][4]
            dve.wait_ge(hi_ready, u + 1)
            dve.tensor_tensor(part(wl, u, w), raw_unit(u), part(wh, u, w).bitcast(F32),
                              ALU.subtract).then_inc(lo_ready, 1)

        def moe_raw(i, q):
            return raw[:, i % RING, q * UNIT:(q + 1) * UNIT]

        def moe_split_hi(act, j, v):
            i, q = divmod(v, TILE // UNIT)
            if q == 0:
                act.wait_ge(slot_loaded[i % RING],
                            16 * (T_MOE // RING + i // RING + 1) + j * (16 * JOB_TILES // RING))
            act.wait_ge(unit_used, j * JOB_UNITS + (U_MOE + v - SPLITS + 1))
            act.activation(wh[:, v % SPLITS, :], moe_raw(i, q), ACT.Copy).then_inc(hi_ready, 1)

        def moe_split_lo(dve, j, v):
            i, q = divmod(v, TILE // UNIT)
            dve.wait_ge(hi_ready, j * JOB_UNITS + (U_MOE + v + 1))
            dve.tensor_tensor(wl[:, v % SPLITS, :], moe_raw(i, q), wh[:, v % SPLITS, :].bitcast(F32),
                              ALU.subtract).then_inc(lo_ready, 1)

        job_steps = [("g", 0), ("u", 0)]
        for i in range(1, SLABS):
            job_steps += [("g", i), ("u", i), ("d", i - 1)]
        job_steps += [("d", SLABS - 1)]

        ROPE_HEADS = 3
        ROPE_PARTS = TT * HEADS // ROPE_HEADS

        def rope_part(eng, link, scratch, which, part_, roped):
            n = ROPE_HEADS
            w = n * HD
            t, h0 = divmod(part_ * n, HEADS)
            c0 = which * QW + h0 * HD
            v = pqk[:, t, c0:c0 + w].rearrange("p (h d) -> p h d", d=HD)
            t1 = scratch[:, 0:w].rearrange("p (h d) -> p h d", d=HD)
            t2 = scratch[:, w:2 * w].rearrange("p (h d) -> p h d", d=HD)
            cos = rope_t[:, 2 * which, t, :]
            sin = rope_t[:, 2 * which + 1, t, :]
            eng.tensor_tensor(t1, v, cos.unsqueeze(1).broadcast_to([P, n, HD]), ALU.mult)
            for a, b in ((0, HH), (HH, 0)):
                ins = eng.tensor_tensor(t2[:, :, a:a + HH], v[:, :, b:b + HH],
                                        sin[:, a:a + HH].unsqueeze(1).broadcast_to([P, n, HH]), ALU.mult)
            link(ins)
            link(eng.tensor_tensor(t1, t1, t2, ALU.add))
            rs = head_sums(HRS, which, t)[:, h0:h0 + n]
            ins = eng.tensor_tensor(v, t1, rs.unsqueeze(2).broadcast_to([P, n, HD]), ALU.mult)
            if part_ == ROPE_PARTS - 1:
                ins.then_inc(roped, 1)
            else:
                link(ins)

        heads_of = [[(n // 4, [g * 4 + n % 4 for g in range(3)]) for n in range(8)],
                    [(n // 4, [6 * (n % 4 // 2) + n % 2 + 2 * g for g in range(3)]) for n in range(8)]]
        score_banks = [(2,), (3,), (0,), (1,), (2, 3), (0, 1), (2, 3), (0, 1)]
        max_before = [0, 0, 0, 0, 2, 4, 5, 6]

        def scores_psum(n):
            b, keys = score_banks[n], P * len(score_banks[n])
            flat = ps[:, b[0]:b[0] + len(b), :].rearrange("p b f -> p (b f)")
            return flat[:, 0:4 * keys].rearrange("p (s k) -> p s k", k=keys)[:, 0:3, :]

        col_tiles = ((0, 1, 2, "g", 3, 4), (0, 1, 2, 3, 4))
        read_act = ((1, 2, 3, 4, 5, 6), (7, 8, 9, 10, 11))

        heads_order = ((0, 0), (0, 1), (1, 0), (1, 1), (0, 2), (1, 2))
        heads_banks = ((4, 5, 6, 7, 0, 1), (7, 0, 1, 2, 4, 5))
        QUARTER_BANKS = (5, 3, 4, 1)
        gain_rows = (R_MIX, R_FFN, R_MIX + KD, R_FFN + KD)
        nblk = sum(w // P for w in widths)
        block_slab = [s for s, w in enumerate(widths) for _ in range(w // P)]
        block_first = [sum(w // P for w in widths[:s]) for s in range(len(widths))]

        block = ctx.enter_context(nc.Block())

        @block.sync
        def _(sp):
            sp.dma_start(xres[:, :, :], x[0].rearrange("(t p) d -> p t d", p=P)).then_inc(x_loaded, 16)
            sp.dma_start(cst[:, :], const_f32).then_inc(const_loaded, 16)
            sp.dma_start(par_rows[R_MIX:R_MIX + 16, :], norm_mix.rearrange("l (k p) -> (l k) p", p=P)).then_inc(par_loaded, 16)
            sp.dma_start(par_rows[R_FFN:R_FFN + 16, :], norm_ffn.rearrange("l (k p) -> (l k) p", p=P)).then_inc(par_loaded, 16)
            sp.dma_start(par_rows[R_BS:R_BS + 4, :], gmlp_bs[0]).then_inc(par_loaded, 16)
            sp.dma_start(par_rows[R_CONV:R_CONV + 6, :], conv_w[0].rearrange("t (k p) -> (t k) p", p=P)).then_inc(par_loaded, 16)
            for t, (src, nrow, ncol) in enumerate(tiles):
                if t >= RING:
                    sp.wait_ge(lo_ready, tile_last[t - RING] + 1)
                dst = raw[:, t % RING, 0:nrow * ncol].rearrange("p (k f) -> p k f", f=ncol)
                if t == 0:
                    h = nrow // 2
                    sp.dma_start(dst[:, 0:h, :], src[:, 0:h, :]).then_inc(first_part_loaded, 16)
                    sp.dma_start(dst[:, h:nrow, :], src[:, h:nrow, :]).then_inc(slot_loaded[0], 16)
                else:
                    sp.dma_start(dst, src).then_inc(slot_loaded[t % RING], 16)
                if t == 0:
                    for src, at_, n in ((dil_q_gain, B_DQ, HD), (dil_k_gain, B_DK, HD), (moba_q_gain, B_MQ, HD),
                                        (moba_k_gain, B_MK, HD), (gmlp_v_gain, B_GV, GW)):
                        sp.dma_start(row_src[0:1, at_:at_ + n], src).then_inc(rows_loaded, 16)
                    sp.dma_start(ws_in[:, :, :], gmlp_ws[0].rearrange("g i j -> i g j")).then_inc(ws_loaded, 16)
                if t == RING - 1:
                    sp.dma_start(router[:, :, :], router_w[0].rearrange("(k p) e -> p k e", p=P)).then_inc(router_loaded, 16)

            def job_loads(e, j, static_first):
                for i, (kind, s) in enumerate(job_steps):
                    if static_first and i < RING:
                        sp.wait_ge(lo_ready, tile_last[T_MOE - RING + i] + 1)
                    else:
                        sp.wait_ge(lo_ready, j * JOB_UNITS + (U_MOE + (i - RING + 1) * (TILE // UNIT)))
                    if kind == "d":
                        src = moe_w_down[0, e, s * SLAB:(s + 1) * SLAB, :]
                        dst = raw[:, i % RING, :].rearrange("p (k f) -> p k f", k=4)
                    else:
                        w = moe_w_gate if kind == "g" else moe_w_up
                        src = w[0, e, :, s * SLAB:(s + 1) * SLAB]
                        dst = raw[:, i % RING, :].rearrange("p (k f) -> p k f", k=KD)
                    if len(src.shape) == 3:
                        src = src.rearrange("o (k p) f -> p (o k) f", p=P)
                    else:
                        src = src.rearrange("(k p) f -> p k f", p=P)
                    sp.dma_start(dst, src).then_inc(slot_loaded[i % RING], 16)

            job_loads(0, 0, True)
            with sp.Fori(1, NE - 1) as j:
                job_loads(bass.ds(j, 1), j, False)
            sp.wait_ge(meta_ready, 1)
            jobs = sp.value_load(meta[0:1, 0:1], min_val=NE, max_val=JOBS_MAX)
            with sp.Fori(NE - 1, jobs) as j:
                e = sp.value_load(meta[0:1, bass.ds(j - (NE - 2), 1)], min_val=0, max_val=NE - 1)
                job_loads(bass.ds(e, 1), j, False)
            sp.wait_ge(lo_ready, jobs * JOB_UNITS + (U_MOE - JOB_UNITS + (2 * RING + 1) * (TILE // UNIT)))
            sp.dma_start(raw[0:1, 0, 0:P], const_f32[0:1, 0:P]).then_inc(slot_loaded[0], 16)
            for n in range(2 * TT):
                half, t = divmod(n, TT)
                cs = slice(half * 512, half * 512 + 512)
                sp.wait_ge(last_added, n + 1)
                sp.dma_start(out[0, t * P:(t + 1) * P, cs], xres[:, t, cs]).then_inc(out_stored, 16)
            sp.wait_ge(out_stored, 16 * 2 * TT)

        @block.gpsimd
        def _(pool):
            pool.wait_ge(ws_loaded, 16)
            pool.affine_select(out=ws_in[:, :, :], in_=ws_in[:, :, :], compare_op=ALU.is_ge, fill=0.0, base=0,
                               pattern=[[0, GG], [-1, P]], channel_multiplier=1).then_inc(ws_masked, 1)
            pool.dma_start(msk[:, :], const_mask).then_inc(masks_loaded, 16)

            n = [0]

            def step(ins):
                n[0] += 1
                ins.then_inc(pool_chain, 1)
                pool.wait_ge(pool_chain, n[0])

            def rope_k(layer):
                pool.wait_ge(head_rstd, layer + 1)
                pool.wait_ge(rope_ready, layer + 1)
                for part_ in range(ROPE_PARTS):
                    rope_part(pool, step, tmp[:, 1, :], 1, part_, k_roped)

            def rope_tables(gq, gk):
                for n, g in enumerate((gq, gk)):
                    gain = rowpar[:, g:g + HD]
                    for half in range(2):
                        lo = half * HH
                        hi = HH - lo
                        last = pool.tensor_tensor(
                            rope_t[:, 2 * n + 1, :, lo:lo + HH],
                            cst[:, C_SIN:C_SIN + TT * HD].rearrange("p (t d) -> p t d", t=TT)[:, :, lo:lo + HH],
                            gain[:, hi:hi + HH].unsqueeze(1).broadcast_to([P, TT, HH]), ALU.mult)
                    last = pool.tensor_tensor(
                        rope_t[:, 2 * n, :, :],
                        cst[:, C_COS:C_COS + TT * HD].rearrange("p (t d) -> p t d", t=TT),
                        gain.unsqueeze(1).broadcast_to([P, TT, HD]), ALU.mult)
                last.then_inc(rope_ready, 1)

            pool.wait_ge(row_ready, 1)
            pool.wait_ge(const_loaded, 16)
            rope_tables(B_DQ, B_DK)
            rope_k(0)
            pool.wait_ge(gv_rstd, 1)
            v = uv[:, :, GW:2 * GW].rearrange("p t (g d) -> p t g d", g=GG)
            for t in range(TT):
                rs = small[:, HRS + t * GG:HRS + (t + 1) * GG]
                step(pool.tensor_tensor(v[:, t], v[:, t], rs.unsqueeze(2).broadcast_to([P, GG, HD]), ALU.mult))
            pool.tensor_tensor(uv[:, :, GW:2 * GW], uv[:, :, GW:2 * GW],
                               rowpar[:, B_GV:B_GV + GW].unsqueeze(1).broadcast_to([P, TT, GW]),
                               ALU.mult).then_inc(gv_ready, 1)
            pool.wait_ge(q_roped, 1)
            pool.wait_ge(k_roped, 1)
            rope_tables(B_MQ, B_MK)
            rope_k(1)

            pool.wait_ge(cv_z, 1)
            pool.wait_ge(cv_copied, 2)
            conv_s = rowpar[:, B_GV:B_GV + SEQ]
            taps = [colpar[:, R_CONV + 2 * t:R_CONV + 2 * t + 2] for t in range(3)]
            for c in range(2):
                step(pool.tensor_scalar(conv_y[:, c, :], conv_z[:, c, :], taps[2][:, c:c + 1], None, ALU.mult))
            for back in (1, 2):
                for c in range(2):
                    step(pool.tensor_scalar(conv_s[:, 0:SEQ - back], conv_z[:, c, 0:SEQ - back],
                                            taps[2 - back][:, c:c + 1], None, ALU.mult))
                    step(pool.tensor_tensor(conv_y[:, c, back:SEQ], conv_y[:, c, back:SEQ],
                                            conv_s[:, 0:SEQ - back], ALU.add))
            pool.tensor_tensor(conv_y[:, :, :], conv_y[:, :, :], conv_b[:, :, :], ALU.mult).then_inc(cv_ready, 1)

            pool.wait_ge(ct_lo, 6)
            pool.memset(rt[:, T_GSLOT:T_GSLOT + 1], 0.0)
            pool.memset(rt[:, T_JP:T_JP + TT * JCOLS], -1.0)
            pool.memset(rt[:, T_JG:T_JG + TT * JCOLS], 0.0).then_inc(zeroed, 1)
            pool.tensor_copy(count_t[:, :, :],
                             cst[:, C_UP:C_UP + 2 * P].rearrange("p (n f) -> p n f", n=2)).then_inc(count_ready, 1)
            pool.memset(pick_t[:, :, :].bitcast(F32), 0.0)
            pool.memset(y_lo[:, :].bitcast(F32), 0.0)
            pool.wait_ge(xs_hi_ready, 1)
            pool.wait_ge(xs_act, 8)
            pool.wait_ge(xs_dve, 8)
            pool.tensor_tensor(xs_lo[:, :, :], xs[:, :, :], xs_hi[:, :, :].bitcast(F32), ALU.subtract).then_inc(xs_lo_ready, 1)
            pool.wait_ge(xs_lo_ready, 1)
            pool.memset(y_hi[:, :].bitcast(F32), 0.0).then_inc(zeroed, 1)

        @block.tensor
        def _(pe):
            def three(out_, sh, sl, mh_, ml_, start, stop):
                pe.matmul(out_, sh, mh_, start=start, stop=False)
                pe.matmul(out_, sh, ml_, start=False, stop=False)
                return pe.matmul(out_, sl, mh_, start=False, stop=stop)

            def setup():
                pe.wait_ge(const_loaded, 16)
                pe.wait_ge(par_loaded, 64)
                pe.transpose(ps[:, 0, 0:R_ROWS], par_rows[0:R_ROWS, :], cst[0:R_ROWS, 0:R_ROWS]).then_inc(setup_pe, 1)

            def setup_rows():
                pe.wait_ge(rows_loaded, 80)
                pe.matmul(bank(4), cst[0:1, C_ONE:C_ONE + P], row_src[0:1, :], start=True, stop=True).then_inc(setup_pe, 1)

            def setup_ws():
                pe.wait_ge(ws_masked, 1)
                for g in range(GG):
                    mm = pe.transpose(ps[:, 5, g * P:(g + 1) * P], ws_in[:, g, :], ident)
                mm.then_inc(setup_pe, 1)

            def norm_T(n):
                for q in range(4):
                    pe.wait_ge(xs_act, 2 * n + q // 2 + 1)
                    pe.wait_ge(xs_dve, 2 * n + q // 2 + 1)
                    for kk in range(2):
                        for t in range(TT):
                            k = 2 * q + kk
                            mm = pe.transpose(ps[:, 4 + q, (kk * TT + t) * P:(kk * TT + t + 1) * P],
                                              xs[:, t, k * P:(k + 1) * P], ident)
                    mm.then_inc(xt_done, 1)

            def project(u0, u1, layer):
                u, c = u0, 0
                while u < u1:
                    t = units[u][0]
                    ncol = tiles[t][2]
                    b = (c % 2) * 2
                    if c == 1 and layer == 0:
                        setup_rows()
                        setup_ws()
                    if c >= 2:
                        pe.wait_ge(proj_act, read_act[layer][c - 2])
                    while u < u1 and units[u][0] == t:
                        _, r0, n, _, w = units[u]
                        pe.wait_ge(lo_ready, u + 1)
                        for r in range(n):
                            k = r0 + r
                            if c == 0 and k % 2 == 0:
                                pe.wait_ge(xt_lo, 8 * layer + k // 2 + 1)
                            for tt in range(TT):
                                sl = slice(tt * P, tt * P + P)
                                mm = three(ps[:, b + tt, 0:ncol], act_hi[:, k, sl], act_lo[:, k, sl],
                                           part(wh, u, w)[:, r, :], part(wl, u, w)[:, r, :], k == 0, k == KD - 1)
                        mm.then_inc(unit_used, 1)
                        u += 1
                    c += 1

            def heads_T(layer):
                pe.wait_ge(q_roped, layer + 1)
                pe.wait_ge(row_ready, 1)
                pe.wait_ge(wsT_ready, 1)
                pe.wait_ge(k_roped, layer + 1)
                for i, (which, b0) in enumerate(heads_order):
                    bank_ = heads_banks[layer][i]
                    if i == (4, 0)[layer]:
                        pe.wait_ge(proj_act, (6, 11)[layer])
                    if layer == 1 and i == 4:
                        pe.wait_ge(cv_copied, 1)
                        pe.wait_ge(cv_z, 1)
                    for bb in range(2):
                        for t in range(TT):
                            blk = 2 * b0 + bb
                            c0 = which * QW + blk * P
                            mm = pe.transpose(ps[:, bank_, (bb * TT + t) * P:(bb * TT + t + 1) * P],
                                              pqk[:, t, c0:c0 + P], ident)
                    mm.then_inc(qkT_done, 1)

            def gmlp():
                pe.wait_ge(gv_ready, 1)
                pe.wait_ge(wsT_ready, 1)
                pe.wait_ge(qkT_dve, 3)
                pe.wait_ge(qkT_act, 3)
                for t in range(TT):
                    for g in range(GG):
                        c = (t * GG + g) * HD
                        mm = pe.matmul(ps[:, 6, c:c + HD], ws_t[:, g, :], uv[:, t, GW + g * HD:GW + (g + 1) * HD],
                                       start=True, stop=True)
                mm.then_inc(gy_done, 1)

            def attention(layer):
                items = heads_of[layer]
                o0 = 8 * layer

                def scores(n):
                    tt, hs = items[n]
                    if max_before[n]:
                        pe.wait_ge(max_ready, o0 + max_before[n])
                    for seg, h in enumerate(hs):
                        lo = (h % 2) * HD
                        mm = pe.matmul(scores_psum(n)[:, seg, :], qT[lo:lo + HD, h // 2, tt * P:(tt + 1) * P],
                                       kT[lo:lo + HD, h // 2, 0:P * (tt + 1)], start=True, stop=True)
                    mm.then_inc(s_done, 1)

                def turn(n):
                    pe.wait_ge(p_ready, o0 + n + 1)
                    if n >= 1:
                        pe.wait_ge(pT_ready, o0 + n)
                    for b in range(3 * (items[n][0] + 1)):
                        mm = pe.transpose(ps[:, 4 + b // 4, (b % 4) * P:(b % 4 + 1) * P],
                                          probs[:, n % 2, b * P:(b + 1) * P], ident)
                    mm.then_inc(pT_done, 1)

                def outputs(n):
                    tt, hs = items[n]
                    pe.wait_ge(pT_ready, o0 + n + 1)
                    if n >= 2:
                        pe.wait_ge(o_ready, o0 + n - 1)
                    if n == 1 and layer == 0:
                        pe.wait_ge(gcat_ready, 1)
                    for seg, h in enumerate(hs):
                        for kb in range(tt + 1):
                            b = seg * (tt + 1) + kb
                            if layer == 0:
                                o = ps[:, 7 - n % 2, 0:HD]
                                st, sp_ = b == 0, b == 3 * (tt + 1) - 1
                            else:
                                o = ps[:, 7 - n % 2, seg * HD:(seg + 1) * HD]
                                st, sp_ = kb == 0, kb == tt
                            mm = pe.matmul(o, probs_t[:, n % 2, b * P:(b + 1) * P],
                                           pv[:, kb, h * HD:(h + 1) * HD], start=st, stop=sp_)
                    mm.then_inc(o_done, 1)

                for n in range(3):
                    if n in (0, 2):
                        ready = 3 * layer + (2 if layer == 1 and n == 0 else 3)
                        pe.wait_ge(qkT_act, ready)
                        pe.wait_ge(qkT_dve, ready)
                    scores(n)
                if layer == 0:
                    gmlp()
                for n in range(8):
                    turn(n)
                    if n >= 1:
                        outputs(n - 1)
                    if n < 5:
                        scores(n + 3)
                if layer == 1:
                    pe.wait_ge(ct_lo, 3)
                    out_units(1, 0, 1)
                outputs(7)
                if layer == 1:
                    out_units(1, 1, 2)

            def cat_T(layer):
                if layer == 1:
                    pe.wait_ge(pT_ready, 16)
                pe.wait_ge(o_ready, 8 * (layer + 1))
                pe.wait_ge(max_ready, 8 * (layer + 1))
                for r in range(2 + layer):
                    for bb in range(2):
                        for t in range(TT):
                            blk = 2 * r + bb
                            src = cat_ab[:, t, blk * P:(blk + 1) * P] if layer == 0 else cat_c[t][:, blk * P:(blk + 1) * P]
                            mm = pe.transpose(ps[:, 4 * layer + r, (bb * TT + t) * P:(bb * TT + t + 1) * P], src, ident)
                    mm.then_inc(ct_done, 1)

            def out_units(layer, n0, n1):
                u0, u1 = (first["out_ab"], first["ffn"]) if layer == 0 else (first["out_cd"], first["moe"])
                for n in range(n0, n1):
                    u = u0 + n
                    k = n if layer == 0 else OUT_CD_ORDER[n]
                    pe.wait_ge(lo_ready, u + 1)
                    for tt in range(TT):
                        for half in range(2):
                            cs = slice(half * 512, half * 512 + 512)
                            sl = slice(tt * P, tt * P + P)
                            mm = three(bank(4 - 4 * layer + 2 * tt + half), act_hi[:, k, sl], act_lo[:, k, sl],
                                       wh[:, u % SPLITS, cs], wl[:, u % SPLITS, cs], n == 0, u == u1 - 1)
                        if u == u1 - 1 and tt == 0:
                            mm.then_inc(sum_done, 1)
                    mm.then_inc(unit_used, 1)

            def ffn():
                u = first["ffn"]
                for s in range(len(widths) + 1):
                    if s < len(widths):
                        for bb in range(widths[s] // P):
                            b = block_first[s] + bb
                            if b >= 4:
                                pe.wait_ge(fh_ready, b - 3)
                            for which in range(2):
                                pe.wait_ge(lo_ready, u + 1)
                                o = ps[:, b % 4, which * SEQ:(which + 1) * SEQ]
                                for k in range(KD):
                                    if b == 0 and which == 0 and k % 2 == 0:
                                        pe.wait_ge(xt_lo, 4 + k // 2 + 1)
                                    mm = three(o, part(wh, u, P)[:, k, :], part(wl, u, P)[:, k, :],
                                               act_hi[:, k, :], act_lo[:, k, :], k == 0, k == KD - 1)
                                mm.then_inc(unit_used, 1)
                                u += 1
                    if s >= 1:
                        for c in range(widths[s - 1] // P):
                            b = block_first[s - 1] + c
                            pe.wait_ge(fh_lo_ready, b + 1)
                            pe.wait_ge(lo_ready, u + 1)
                            for tt in range(TT):
                                for half in range(2):
                                    cs = slice(half * 512, half * 512 + 512)
                                    sl = slice(tt * P, tt * P + P)
                                    mm = three(bank(4 + 2 * tt + half), fh_hi[:, (s - 1) % 2, c, sl],
                                               fh_lo[:, (s - 1) % 2, c, sl], wh[:, u % SPLITS, cs],
                                               wl[:, u % SPLITS, cs], b == 0, b == nblk - 1)
                                if b == nblk - 1 and tt == 0:
                                    mm.then_inc(sum_done, 1)
                            mm.then_inc(unit_used, 1)
                            u += 1

            def conv_projection():
                for z in range(3):
                    for c in range(2):
                        u = first["conv"] + 2 * z + c
                        pe.wait_ge(lo_ready, u + 1)
                        o = ps[:, 4 + z, c * SEQ:(c + 1) * SEQ]
                        for k in range(KD):
                            mm = three(o, part(wh, u, P)[:, k, :], part(wl, u, P)[:, k, :],
                                       act_hi[:, k, :], act_lo[:, k, :], k == 0, k == KD - 1)
                        mm.then_inc(unit_used, 1)

            setup()
            norm_T(0)
            project(0, first["out_ab"], 0)
            heads_T(0)
            attention(0)
            cat_T(0)
            pe.wait_ge(ct_lo, 2)
            pe.wait_ge(pT_ready, 8)
            out_units(0, 0, 4)
            norm_T(1)
            ffn()
            norm_T(2)
            project(first["in_cd"], first["conv"], 1)
            conv_projection()
            heads_T(1)
            pe.wait_ge(cv_copied, 2)
            attention(1)
            cat_T(1)
            pe.wait_ge(ct_lo, 6)
            out_units(1, 2, 8)
            norm_T(3)
            pe.wait_ge(router_lo_ready, 1)
            for tt in range(TT):
                for k in range(KD):
                    if tt == 0 and k % 2 == 0:
                        pe.wait_ge(xt_lo, 12 + k // 2 + 1)
                    sl = slice(tt * P, tt * P + P)
                    o = ps[:, 0, tt * 2 * NE:(tt + 1) * 2 * NE]
                    pe.matmul(o, act_hi[:, k, sl], router_hl[:, k, :, :].rearrange("p h e -> p (h e)"),
                              start=k == 0, stop=False)
                    mm = pe.matmul(o[:, 0:NE], act_lo[:, k, sl], router_hl[:, k, 0, :], start=False, stop=k == KD - 1)
            mm.then_inc(lg_done, 1)
            pe.wait_ge(sel_ready, 1)
            pe.wait_ge(count_ready, 1)
            sel = [sel_b[:, t, :] for t in range(TT)]
            up, ones = count_t[:, 0, :], count_t[:, 1, :]
            pe.matmul(ps[:, 1, 0:8], up, sel[0], start=True, stop=True)
            pe.matmul(ps[:, 1, 8:16], ones, sel[0], start=True, stop=False)
            pe.matmul(ps[:, 1, 8:16], up, sel[1], start=False, stop=True)
            pe.matmul(ps[:, 1, 16:24], ones, sel[0], start=True, stop=False)
            pe.matmul(ps[:, 1, 16:24], ones, sel[1], start=False, stop=True).then_inc(cnt_done, 1)

            def gather(j1):
                pe.wait_ge(xs_lo_ready, 1)
                pe.wait_ge(pick_ready, j1 + 1)
                for k in range(KD):
                    o = ps[:, 1 if k < 4 else 3, (k % 4) * P:(k % 4 + 1) * P]
                    for t in range(TT):
                        pe.matmul(o, xs_hi[:, t, k * P:(k + 1) * P], pick[:, t, :], start=t == 0, stop=False)
                        mm = pe.matmul(o, xs_lo[:, t, k * P:(k + 1) * P], pick[:, t, :], start=False, stop=t == TT - 1)
                    if k % 4 == 3:
                        mm.then_inc(gather_done, 1)

            def combine(j):
                pe.wait_ge(y_dve, 2 * j + 2)
                pe.wait_ge(xg_lo_ready, 2 * j + 2)
                for n, b in enumerate((5, 4, 3, 1)):
                    t, half = divmod(n, 2)
                    cs = slice(half * 512, half * 512 + 512)
                    pe.matmul(bank(b), pick_t[:, t, :], y_hi[:, cs], start=True, stop=False)
                    mm = pe.matmul(bank(b), pick_t[:, t, :], y_lo[:, cs], start=False, stop=True)
                mm.then_inc(comb_done, 1)

            def transpose_h(j, i):
                pe.wait_ge(h_ready, SLABS * j + (i + 1))
                if i >= 1:
                    pe.wait_ge(hT_lo, SLABS * j + i)
                for c in range(4):
                    mm = pe.transpose(ps[:, 4, c * P:(c + 1) * P], mh[:, i % 2, c * P:(c + 1) * P], ident)
                mm.then_inc(hT_done, 1)

            pe.wait_ge(zeroed, 2)
            for half in range(2):
                mm = pe.matmul(bank(6 + half), pick_t[:, 0, :], y_hi[:, 0:512], start=True, stop=True)
            mm.then_inc(y_zeroed, 1)
            gather(0)
            pe.wait_ge(meta_ready, 1)
            jobs = pe.value_load(meta[0:1, 0:1], min_val=NE, max_val=JOBS_MAX)
            with pe.Fori(0, jobs) as j:
                for v, (kind, i) in enumerate(job_steps):
                    if kind == "g" and i == 1:
                        pe.wait_ge(comb_added, j + 1)
                    if kind == "g" and i >= 2:
                        pe.wait_ge(silu_ready, SLABS * j + (i - 1))
                    if kind == "u" and i >= 2:
                        pe.wait_ge(h_ready, SLABS * j + (i - 1))
                    if kind == "d" and i == 0:
                        pe.wait_ge(y_dve, 2 * j + 2)
                    if kind == "d":
                        pe.wait_ge(hT_lo, SLABS * j + (i + 1))
                    for q in range(4):
                        w = 4 * v + q
                        pe.wait_ge(lo_ready, j * JOB_UNITS + (U_MOE + w + 1))
                        if v == 0 and q % 2 == 0:
                            pe.wait_ge(xg_lo_ready, 2 * j + (q // 2 + 1))
                        if kind == "d":
                            for half in range(2):
                                cs = slice(half * 512, half * 512 + 512)
                                mm = three(bank(6 + half), mh_hi[:, q, :], mh_lo[:, q, :], wh[:, w % SPLITS, cs],
                                           wl[:, w % SPLITS, cs], i == 0 and q == 0, i == SLABS - 1 and q == 3)
                        else:
                            b = (0 if kind == "g" else 2) + i % 2
                            for r in range(2):
                                k = 2 * q + r
                                cs = slice(r * 512, r * 512 + 512)
                                mm = three(bank(b), xg_hi[:, k, :], xg_lo[:, k, :], wh[:, w % SPLITS, cs],
                                           wl[:, w % SPLITS, cs], k == 0, k == KD - 1)
                        mm.then_inc(unit_used, 1)
                    if kind == "g" and i == 0:
                        combine(j)
                    if kind == "g" and i >= 1:
                        transpose_h(j, i - 1)
                    if kind == "g" and i == 2:
                        for t in range(TT):
                            pe.transpose(ps[:, 5, t * P:(t + 1) * P], pick[:, t, :].bitcast(F32), ident)
                        for t in range(TT):
                            mm = pe.matmul(ps[:, 5, TT * P:TT * P + 1], pick[:, t, :].bitcast(F32),
                                           rt[:, T_GTOK + t:T_GTOK + t + 1], start=t == 0, stop=t == TT - 1)
                        mm.then_inc(pickT_done, 1)
                    if kind == "d" and i == SLABS - 2:
                        transpose_h(j, SLABS - 1)
                        gather(j + 1)
            pe.wait_ge(xg_lo_ready, 2 * jobs + 2)
            for half in range(2):
                pe.wait_ge(y_dve, 2 * jobs + (half + 1))
                cs = slice(half * 512, half * 512 + 512)
                for t in range(TT):
                    o = bank(QUARTER_BANKS[half * TT + t])
                    pe.matmul(o, pick_t[:, t, :], y_hi[:, cs], start=True, stop=False)
                    pe.matmul(o, pick_t[:, t, :], y_lo[:, cs], start=False, stop=True).then_inc(last_done, 1)

        @block.scalar
        def _(act):
            def norm(n):
                act.preload_act_table(ACT.Sqrt)
                if n == 0:
                    act.wait_ge(x_loaded, 16)
                else:
                    act.wait_ge(res_added, 2 * n - 1)
                act.activation(xs[:, 0, :], xres[:, 0, :], ACT.Square, accum_out=small[:, SS:SS + 1]).then_inc(sq_act, 1)
                act.wait_ge(ms_ready, n + 1)
                act.activation(small[:, SD:SD + 2], small[:, MS:MS + 2], ACT.Sqrt).then_inc(std_ready, 1)
                act.wait_ge(rstd_ready, n + 1)
                for half in range(2):
                    cs = slice(half * 512, half * 512 + 512)
                    act.activation(xs[:, 0, cs], xres[:, 0, cs], ACT.Copy, scale=small[:, RS:RS + 1]).then_inc(xs_act, 1)
                if n == 0:
                    act.wait_ge(col_ready, 1)
                elif n < 3:
                    split_hi(act, (first["ffn"] if n == 1 else first["in_cd"]) - 1 + SPLITS)
                for q in range(4):
                    act.wait_ge(xt_done, 4 * n + q + 1)
                    for kk in range(2):
                        k = 2 * q + kk
                        g = gain_rows[n] + k
                        ins = act.activation(act_hi[:, k, :], ps[:, 4 + q, kk * SEQ:(kk + 1) * SEQ], ACT.Copy,
                                             scale=colpar[:, g:g + 1])
                    ins.then_inc(xt_hi, 1)
                    if n == 0 and q == 1:
                        split_hi(act, 0)

            def project(u0, u1, layer):
                u, c = u0, 0
                while u < u1:
                    t = units[u][0]
                    ncol = tiles[t][2]
                    b = (c % 2) * 2
                    while u < u1 and units[u][0] == t:
                        split_hi(act, u + SPLITS)
                        u += 1
                    act.wait_ge(unit_used, u)
                    m = col_tiles[layer][c]
                    if m == "g":
                        act.activation(uv[:, 0, :], bank(b), ACT.Gelu_apprx_tanh)
                        act.activation(uv[:, 1, :], bank(b + 1), ACT.Gelu_apprx_tanh).then_inc(proj_act, 1)
                    else:
                        dst = pqk[:, :, m * 512:m * 512 + ncol] if m < 3 else pv[:, :, (m - 3) * 512:(m - 3) * 512 + ncol]
                        act.activation(dst, ps[:, b:b + TT, 0:ncol], ACT.Copy).then_inc(proj_act, 1)
                    if c == 1 and layer == 0:
                        act.wait_ge(setup_pe, 3)
                        act.activation(ws_t[:, :, :], ps[:, 5, :].rearrange("p (g f) -> p g f", g=GG),
                                       ACT.Copy).then_inc(wsT_ready, 1)
                    if m in (1, 2):
                        act.wait_ge(proj_act, read_act[layer][c])
                        for r in range(2):
                            n = 4 * layer + 2 * (m - 1) + r
                            if n >= 1:
                                act.wait_ge(sq_used, n)
                            if n == 4:
                                act.wait_ge(q_roped, 1)
                                act.wait_ge(k_roped, 1)
                            c0 = (m - 1) * QW + r * 6 * HD
                            act.activation(tmp[:, :, :], pqk[:, :, c0:c0 + 6 * HD], ACT.Square).then_inc(sq_ready, 1)
                    if m == 2:
                        act.wait_ge(head_ms, layer + 1)
                        act.activation(small[:, HSD + 8:HSD + HN], small[:, HMS + 8:HMS + HN],
                                       ACT.Sqrt).then_inc(head_std, 1)
                        act.preload_act_table(ACT.Exp if layer else ACT.Gelu_apprx_tanh)
                    if m == 3 and layer == 0:
                        act.wait_ge(gv_ms, 1)
                        act.activation(small[:, HSD:HSD + 8], small[:, HMS:HMS + 8], ACT.Sqrt).then_inc(gv_std, 1)
                        act.preload_act_table(ACT.Exp)
                    c += 1

            def heads_T(layer):
                for i in (0, 2, 4):
                    which, b0 = heads_order[i]
                    act.wait_ge(qkT_done, 6 * layer + i + 1)
                    act.activation((qT, kT)[which][:, 2 * b0:2 * b0 + 2, :],
                                   ps[:, heads_banks[layer][i], :].rearrange("p (b f) -> p b f", b=2), ACT.Copy).then_inc(qkT_act, 1)

            def attention(layer):
                o0 = 8 * layer
                for n in range(9):
                    if n < 8:
                        tt, hs = heads_of[layer][n]
                        keys = P * (tt + 1)
                        act.wait_ge(max_ready, o0 + n + 1)
                        for seg in range(3 if layer else 1):
                            w = keys if layer else 3 * keys
                            v = probs[:, n % 2, seg * w:(seg + 1) * w]
                            c = 3 * n + seg
                            ins = act.activation(v, v, ACT.Exp, bias=small[:, NM + c:NM + c + 1],
                                                 accum_out=small[:, LS + c:LS + c + 1])
                        ins.then_inc(p_ready, 1)
                    if n >= 1:
                        m = n - 1
                        nb = 3 * (heads_of[layer][m][0] + 1)
                        act.wait_ge(pT_done, o0 + m + 1)
                        if m >= 2:
                            act.wait_ge(o_done, o0 + m - 1)
                        act.activation(probs_t[:, m % 2, 0:nb * P],
                                       ps[:, 4:6, :].rearrange("p b f -> p (b f)")[:, 0:nb * P],
                                       ACT.Copy).then_inc(pT_ready, 1)
                    if n == 7 and layer == 1:
                        act.wait_ge(cv_ready, 1)
                        act.wait_ge(s_done, 16)
                        act.activation(act_hi[:, 6:8, :], conv_y[:, :, :], ACT.Copy).then_inc(ct_hi, 1)

            def cat_T(layer):
                for r in range(2 + layer):
                    act.wait_ge(ct_done, 2 * layer + r + 1)
                    act.activation(act_hi[:, 2 * r:2 * r + 2, :],
                                   ps[:, 4 * layer + r, :].rearrange("p (b f) -> p b f", b=2), ACT.Copy).then_inc(ct_hi, 1)

            def ffn():
                u = first["ffn"]
                for s in range(len(widths) + 1):
                    if s < len(widths):
                        for bb in range(widths[s] // P):
                            b = block_first[s] + bb
                            split_hi(act, u + SPLITS)
                            split_hi(act, u + 1 + SPLITS)
                            u += 2
                            act.wait_ge(unit_used, u)
                            if b >= 2:
                                act.wait_ge(fh_ready, b - 1)
                            act.activation(fsg[:, b % 2, :], ps[:, b % 4, 0:SEQ], ACT.Silu).then_inc(fsg_ready, 1)
                            act.wait_ge(fh_ready, b + 1)
                            act.activation(fh_hi[:, s % 2, bb, :], fh[:, b % 2, :], ACT.Copy).then_inc(fh_hi_ready, 1)
                    if s >= 1:
                        for c in range(widths[s - 1] // P):
                            if u < first["in_cd"] - 1:
                                split_hi(act, u + SPLITS)
                            u += 1

            norm(0)
            for u in range(1, SPLITS):
                split_hi(act, u)
            project(0, first["out_ab"], 0)
            heads_T(0)
            attention(0)
            cat_T(0)
            for u in range(first["out_ab"], first["ffn"] - 1):
                split_hi(act, u + SPLITS)
            act.wait_ge(router_loaded, 16)
            act.activation(router_hl[:, :, 0, :], router[:, :, :], ACT.Copy).then_inc(router_hi_ready, 1)
            norm(1)
            act.preload_act_table(ACT.Silu)
            ffn()
            norm(2)
            project(first["in_cd"], first["conv"], 1)
            for z in range(3):
                for c in range(2):
                    split_hi(act, first["conv"] + 2 * z + c + SPLITS)
                act.wait_ge(unit_used, first["conv"] + 2 * z + 2)
                if z != 1:
                    act.activation(conv_z[:, :, :] if z == 0 else conv_b[:, :, :],
                                   ps[:, 4 + z, :].rearrange("p (c f) -> p c f", c=2), ACT.Copy).then_inc(cv_copied, 1)
            heads_T(1)
            attention(1)
            cat_T(1)
            for u in range(first["out_cd"], first["moe"]):
                split_hi(act, u + SPLITS)
            norm(3)
            act.wait_ge(xs_act, 8)
            act.wait_ge(xs_dve, 8)
            act.activation(xs_hi[:, :, :], xs[:, :, :], ACT.Copy).then_inc(xs_hi_ready, 1)
            act.preload_act_table(ACT.Exp)
            act.wait_ge(diff_ready, 1)
            act.activation(rt[:, T_EXP:T_EXP + 2], rt[:, T_DIFF:T_DIFF + 2], ACT.Exp).then_inc(exp_ready, 1)
            act.preload_act_table(ACT.Silu)

            def gathered(j1):
                for k in range(KD):
                    if k % 4 == 0:
                        act.wait_ge(gather_done, 2 * j1 + (k // 4 + 1))
                    g = gain_rows[3] + k
                    ins = act.activation(xg_hi[:, k, :], ps[:, 1 if k < 4 else 3, (k % 4) * P:(k % 4 + 1) * P], ACT.Copy,
                                         scale=colpar[:, g:g + 1])
                    if k % 4 == 3:
                        ins.then_inc(xg_hi_ready, 1)

            def turned_h(j, i):
                act.wait_ge(hT_done, SLABS * j + (i + 1))
                act.activation(mh_hi[:, :, :], ps[:, 4, :].rearrange("p (c f) -> p c f", c=4), ACT.Copy).then_inc(hT_hi, 1)

            def y_out(j):
                act.wait_ge(unit_used, j * JOB_UNITS + U_MOE)
                for half in range(2):
                    act.activation(y_hi[:, half * 512:(half + 1) * 512], bank(6 + half), ACT.Copy,
                                   scale=rt[:, T_GSLOT:T_GSLOT + 1]).then_inc(y_act, 1)

            for w in range(SPLITS - 1):
                moe_split_hi(act, 0, w)
            gathered(0)
            act.wait_ge(y_zeroed, 1)
            act.wait_ge(meta_ready, 1)
            jobs = act.value_load(meta[0:1, 0:1], min_val=NE, max_val=JOBS_MAX)
            with act.Fori(0, jobs) as j:
                y_out(j)
                moe_split_hi(act, j, SPLITS - 1)
                for v, (kind, i) in enumerate(job_steps):
                    for w in range(4 * v + SPLITS, min(4 * v + 4 + SPLITS, JOB_UNITS + SPLITS - 1)):
                        moe_split_hi(act, j, w)
                    if kind == "g":
                        act.wait_ge(unit_used, j * JOB_UNITS + (U_MOE + 4 * v + 4))
                        if i >= 2:
                            act.wait_ge(h_ready, SLABS * j + (i - 1))
                        act.activation(msg[:, i % 2, :], bank(i % 2), ACT.Silu).then_inc(silu_ready, 1)
                        if i >= 1:
                            turned_h(j, i - 1)
                        if i == 2:
                            act.wait_ge(pickT_done, j + 1)
                            act.activation(pick_t[:, :, :], ps[:, 5, 0:TT * P].rearrange("p (t f) -> p t f", t=TT), ACT.Copy)
                            act.activation(rt[:, T_GSLOT:T_GSLOT + 1], ps[:, 5, TT * P:TT * P + 1],
                                           ACT.Copy).then_inc(pickT_ready, 1)
                    if kind == "d" and i == SLABS - 2:
                        turned_h(j, SLABS - 1)
                        gathered(j + 1)
            y_out(jobs)

        @block.vector
        def _(dve):
            chain = [0]

            def link(ins):
                chain[0] += 1
                ins.then_inc(dve_chain, 1)
                dve.wait_ge(dve_chain, chain[0])

            def norm(n):
                if n == 0:
                    dve.wait_ge(x_loaded, 16)
                else:
                    dve.wait_ge(res_added, 2 * n)
                link(dve.tensor_tensor_reduce(xs[:, 1, :], xres[:, 1, :], xres[:, 1, :], 1.0, 0.0, ALU.mult, ALU.add,
                                              small[:, SS + 1:SS + 2]))
                dve.wait_ge(sq_act, n + 1)
                dve.tensor_scalar(small[:, MS:MS + 2], small[:, SS:SS + 2], 1.0 / D, EPS, ALU.mult,
                                  ALU.add).then_inc(ms_ready, 1)
                dve.wait_ge(std_ready, n + 1)
                dve.reciprocal(small[:, RS:RS + 2], small[:, SD:SD + 2]).then_inc(rstd_ready, 1)
                dve.wait_ge(rstd_ready, n + 1)
                for half in range(2):
                    cs = slice(half * 512, half * 512 + 512)
                    dve.tensor_scalar(xs[:, 1, cs], xres[:, 1, cs], small[:, RS + 1:RS + 2], None,
                                      ALU.mult).then_inc(xs_dve, 1)
                if n in (1, 2):
                    split_lo(dve, (first["ffn"] if n == 1 else first["in_cd"]) - 1 + SPLITS)
                if n == 0:
                    dve.wait_ge(setup_pe, 1)
                    dve.tensor_copy(colpar[:, 0:R_ROWS], ps[:, 0, 0:R_ROWS]).then_inc(col_ready, 1)
                    dve.wait_ge(col_ready, 1)
                for q in range(4):
                    dve.wait_ge(xt_hi, 4 * n + q + 1)
                    for kk in range(2):
                        k = 2 * q + kk
                        g = gain_rows[n] + k
                        ins = dve.scalar_tensor_tensor(
                            out=act_lo[:, k, :], in0=ps[:, 4 + q, kk * SEQ:(kk + 1) * SEQ], scalar=colpar[:, g:g + 1],
                            in1=act_hi[:, k, :].bitcast(F32), op0=ALU.mult, op1=ALU.subtract)
                    ins.then_inc(xt_lo, 1)
                    if n == 0 and q == 1:
                        split_lo(dve, 0)

            def group_sums(src, heads, dst):
                sq = tmp[:, 0, 0:heads * HD]
                link(dve.tensor_tensor(sq, src, src, ALU.mult))
                link(dve.tensor_reduce(dst, sq.rearrange("p (h d) -> p h d", d=HD), AX.X, ALU.add))

            roped = [None]

            def rope_next():
                if roped[0] is not None and roped[0] < ROPE_PARTS:
                    rope_part(dve, link, tmp[:, 0, :], 0, roped[0], q_roped)
                    roped[0] += 1

            def project(u0, u1, layer):
                u, c = u0, 0
                while u < u1:
                    t = units[u][0]
                    ncol = tiles[t][2]
                    b = (c % 2) * 2
                    while u < u1 and units[u][0] == t:
                        if layer == 1 or u + SPLITS < first["out_ab"]:
                            split_lo(dve, u + SPLITS)
                        u += 1
                        rope_next()
                    m = col_tiles[layer][c]
                    if c == 1 and layer == 0:
                        dve.wait_ge(setup_pe, 2)
                        for c_ in (B_DQ, B_MQ):
                            dve.tensor_scalar(rowpar[:, c_:c_ + HD], ps[:, 4, c_:c_ + HD], QSCALE, None, ALU.mult)
                        dve.tensor_copy(rowpar[:, B_DK:B_DK + HD], ps[:, 4, B_DK:B_DK + HD])
                        dve.tensor_copy(rowpar[:, B_MK:512], ps[:, 4, B_MK:512]).then_inc(row_ready, 1)
                    dve.wait_ge(proj_act, read_act[layer][c])
                    if m == "g":
                        for t_ in range(TT):
                            group_sums(uv[:, t_, GW:2 * GW], GG, small[:, HSS + t_ * GG:HSS + (t_ + 1) * GG])
                        dve.tensor_scalar(small[:, HMS:HMS + 8], small[:, HSS:HSS + 8], 1.0 / HD, EPS,
                                          ALU.mult, ALU.add).then_inc(gv_ms, 1)
                    if m in (1, 2):
                        for r in range(2):
                            dve.wait_ge(sq_ready, 4 * layer + 2 * (m - 1) + r + 1)
                            at_ = HSS + 8 + (m - 1) * TT * HEADS
                            sums = small[:, at_:at_ + TT * HEADS].rearrange("p (t h) -> p t h", t=TT)
                            dve.tensor_reduce(sums[:, :, 6 * r:6 * r + 6], tmp[:, :, :].rearrange("p t (h d) -> p t h d", d=HD),
                                              AX.X, ALU.add).then_inc(sq_used, 1)
                    if m == 2:
                        dve.wait_ge(sq_used, 4 * layer + 4)
                        dve.tensor_scalar(small[:, HMS + 8:HMS + HN], small[:, HSS + 8:HSS + HN], 1.0 / HD, EPS,
                                          ALU.mult, ALU.add).then_inc(head_ms, 1)
                        dve.wait_ge(head_std, layer + 1)
                        dve.reciprocal(small[:, HRS + 8:HRS + HN], small[:, HSD + 8:HSD + HN]).then_inc(head_rstd, 1)
                        dve.wait_ge(head_rstd, layer + 1)
                        dve.wait_ge(rope_ready, layer + 1)
                        roped[0] = 0
                    if m == 3 and layer == 0:
                        dve.wait_ge(gv_std, 1)
                        dve.reciprocal(small[:, HRS:HRS + 8], small[:, HSD:HSD + 8]).then_inc(gv_rstd, 1)
                    c += 1

            def heads_T(layer):
                for i in (1, 3, 5):
                    which, b0 = heads_order[i]
                    dve.wait_ge(qkT_done, 6 * layer + i + 1)
                    dve.tensor_copy((qT, kT)[which][:, 2 * b0:2 * b0 + 2, :],
                                    ps[:, heads_banks[layer][i], :].rearrange("p (b f) -> p b f", b=2)).then_inc(qkT_dve, 1)

            def attention(layer):
                o0 = 8 * layer
                dve.wait_ge(masks_loaded, 16)
                for n in range(10):
                    if n < 8:
                        tt, hs = heads_of[layer][n]
                        keys = P * (tt + 1)
                        dve.wait_ge(s_done, o0 + n + 1)
                        if n >= 2:
                            dve.wait_ge(pT_done, o0 + n - 1)
                        if layer == 0:
                            m0 = (M_DIL0, M_DIL1)[tt]
                            link(dve.tensor_tensor_reduce(
                                probs[:, n % 2, 0:3 * keys].rearrange("p (s k) -> p s k", s=3), scores_psum(n),
                                msk[:, m0:m0 + 3 * keys].rearrange("p (s k) -> p s k", s=3), 1.0, NEG, ALU.add, ALU.max,
                                small[:, MX + 3 * n:MX + 3 * n + 1]))
                            dve.tensor_scalar(small[:, NM + 3 * n:NM + 3 * n + 1], small[:, MX + 3 * n:MX + 3 * n + 1],
                                              -1.0, None, ALU.mult).then_inc(max_ready, 1)
                        else:
                            m0 = M_CAUSAL + P - tt * P
                            for seg in range(3):
                                ins = dve.tensor_tensor_reduce(
                                    probs[:, n % 2, seg * keys:(seg + 1) * keys], scores_psum(n)[:, seg, :],
                                    msk[:, m0:m0 + keys], 1.0, NEG, ALU.add, ALU.max,
                                    small[:, MX + 3 * n + seg:MX + 3 * n + seg + 1])
                            link(ins)
                            dve.tensor_scalar(small[:, NM + 3 * n:NM + 3 * n + 3], small[:, MX + 3 * n:MX + 3 * n + 3],
                                              -1.0, None, ALU.mult).then_inc(max_ready, 1)
                    if 2 <= n < 2 + SPLITS:
                        split_lo(dve, first[("out_ab", "out_cd")[layer]] + n - 2)
                    if n == 1 and layer == 0:
                        dve.wait_ge(gy_done, 1)
                        y = ps[:, 6, :].rearrange("p (t g d) -> p t g d", t=TT, g=GG)
                        for g in range(GG):
                            ins = dve.scalar_tensor_tensor(
                                out=cat_ab[:, :, g * HD:(g + 1) * HD], in0=y[:, :, g, :],
                                scalar=colpar[:, R_BS + g:R_BS + g + 1], in1=uv[:, :, g * HD:(g + 1) * HD],
                                op0=ALU.add, op1=ALU.mult)
                        ins.then_inc(gcat_ready, 1)
                    if n == 8 and layer == 1:
                        dve.wait_ge(ct_hi, 3)
                        dve.tensor_tensor(act_lo[:, 6:8, :], conv_y[:, :, :], act_hi[:, 6:8, :].bitcast(F32),
                                          ALU.subtract).then_inc(ct_lo, 1)
                    if n >= 2:
                        m = n - 2
                        tt, hs = heads_of[layer][m]
                        ns = 3 if layer else 1
                        c = 3 * m
                        dve.wait_ge(p_ready, o0 + m + 1)
                        link(dve.reciprocal(small[:, RL + c:RL + c + ns], small[:, LS + c:LS + c + ns]))
                        dve.wait_ge(o_done, o0 + m + 1)
                        if layer == 0:
                            d0 = GW + (m % 4) * HD
                            dve.tensor_scalar(cat_ab[:, tt, d0:d0 + HD], ps[:, 7 - m % 2, 0:HD], small[:, RL + c:RL + c + 1],
                                              None, ALU.mult).then_inc(o_ready, 1)
                        else:
                            if m == 4:
                                dve.wait_ge(cv_ready, 1)
                            d0 = (hs[0] - hs[0] % 2) * HD
                            dst = cat_c[tt][:, d0:d0 + 6 * HD].rearrange("p (s d) -> p s d", s=3)
                            dve.tensor_tensor(dst[:, :, (hs[0] % 2) * HD:(hs[0] % 2 + 1) * HD],
                                              ps[:, 7 - m % 2, 0:3 * HD].rearrange("p (s d) -> p s d", s=3),
                                              small[:, RL + c:RL + c + 3].unsqueeze(2).broadcast_to([P, 3, HD]),
                                              ALU.mult).then_inc(o_ready, 1)

            def cat_T(layer):
                for r in range(2 + layer):
                    dve.wait_ge(ct_hi, 3 * layer + r + 1)
                    dve.tensor_tensor(act_lo[:, 2 * r:2 * r + 2, :], ps[:, 4 * layer + r, :].rearrange("p (b f) -> p b f", b=2),
                                      act_hi[:, 2 * r:2 * r + 2, :].bitcast(F32), ALU.subtract).then_inc(ct_lo, 1)

            def residual(n, u_end):
                for t in range(TT):
                    if t == 0:
                        dve.wait_ge(sum_done, n + 1)
                    else:
                        dve.wait_ge(unit_used, u_end)
                    for half in range(2):
                        v = xres[:, t, half * 512:(half + 1) * 512]
                        ins = dve.tensor_tensor(v, v, bank((0 if n == 2 else 4) + 2 * t + half), ALU.add)
                    ins.then_inc(res_added, 1)

            def ffn():
                u = first["ffn"]
                for s in range(len(widths) + 1):
                    if s < len(widths):
                        for bb in range(widths[s] // P):
                            b = block_first[s] + bb
                            split_lo(dve, u + SPLITS)
                            split_lo(dve, u + 1 + SPLITS)
                            u += 2
                            dve.wait_ge(fsg_ready, b + 1)
                            dve.tensor_tensor(fh[:, b % 2, :], fsg[:, b % 2, :], ps[:, b % 4, SEQ:2 * SEQ],
                                              ALU.mult).then_inc(fh_ready, 1)
                            dve.wait_ge(fh_hi_ready, b + 1)
                            dve.tensor_tensor(fh_lo[:, s % 2, bb, :], fh[:, b % 2, :], fh_hi[:, s % 2, bb, :].bitcast(F32),
                                              ALU.subtract).then_inc(fh_lo_ready, 1)
                    if s >= 1:
                        for c in range(widths[s - 1] // P):
                            if u < first["in_cd"] - 1:
                                split_lo(dve, u + SPLITS)
                            u += 1

            norm(0)
            for u in range(1, SPLITS):
                split_lo(dve, u)
            project(0, first["out_ab"], 0)
            heads_T(0)
            attention(0)
            cat_T(0)
            for u in range(first["out_ab"], first["ffn"] - 1):
                split_lo(dve, u + SPLITS)
            residual(0, first["ffn"])
            norm(1)
            dve.wait_ge(router_hi_ready, 1)
            dve.tensor_tensor(router_hl[:, :, 1, :], router[:, :, :], router_hl[:, :, 0, :].bitcast(F32),
                              ALU.subtract).then_inc(router_lo_ready, 1)
            ffn()
            residual(1, first["in_cd"])
            norm(2)
            project(first["in_cd"], first["conv"], 1)
            for z in range(3):
                for c in range(2):
                    u = first["conv"] + 2 * z + c + SPLITS
                    if u < first["out_cd"]:
                        split_lo(dve, u)
                    rope_next()
                if z == 1:
                    dve.wait_ge(unit_used, first["conv"] + 4)
                    dve.wait_ge(cv_copied, 1)
                    dve.tensor_tensor(conv_z[:, :, :], conv_z[:, :, :], ps[:, 5, :].rearrange("p (c f) -> p c f", c=2),
                                      ALU.mult).then_inc(cv_z, 1)
            heads_T(1)
            attention(1)
            cat_T(1)
            for u in range(first["out_cd"], first["moe"]):
                split_lo(dve, u + SPLITS)
            residual(2, first["moe"])
            norm(3)

            def r(c, n=1):
                return rt[:, c:c + n]

            def r2(c):
                return rt[:, c:c + TT * NE]

            dve.wait_ge(zeroed, 1)
            dve.wait_ge(lg_done, 1)
            lg2 = ps[:, 0, 0:2 * TT * NE].rearrange("p (t h e) -> p t h e", t=TT, h=2)
            lgv = r2(T_LG).rearrange("p (t e) -> p t e", t=TT)
            link(dve.tensor_copy(lgv, lg2[:, :, 0, :]))
            link(dve.tensor_tensor(lgv, lgv, lg2[:, :, 1, :], ALU.add))
            for t in range(TT):
                ins = dve.max(r(T_MX + t * NE, NE), r(T_LG + t * NE, NE))
            link(ins)
            mx = r2(T_MX).rearrange("p (t e) -> p t e", t=TT)
            dve.tensor_tensor(r(T_DIFF, TT).unsqueeze(2), mx[:, :, 1:2], mx[:, :, 0:1], ALU.subtract).then_inc(diff_ready, 1)
            other = lgv.unsqueeze(2).broadcast_to([P, TT, NE, NE])
            own = lgv.unsqueeze(3).broadcast_to([P, TT, NE, NE])
            lower = cst[:, C_LT:C_LT + 64].rearrange("p (e f) -> p e f", e=NE).unsqueeze(1).broadcast_to([P, TT, NE, NE])
            c1, c2 = (r(at_, TT * 64).rearrange("p (t e f) -> p t e f", t=TT, e=NE) for at_ in (T_CMP, T_CMP2))
            dve.tensor_tensor(c1, other, own, ALU.is_gt)
            link(dve.tensor_tensor(c2, other, own, ALU.is_equal))
            link(dve.tensor_tensor(c2, c2, lower, ALU.mult))
            link(dve.tensor_tensor(c1, c1, c2, ALU.add))
            link(dve.tensor_reduce(r2(T_RANK).rearrange("p (t e) -> p t e", t=TT), c1, AX.X, ALU.add))
            dve.tensor_scalar(sel_b[:, :, :].rearrange("p t e -> p (t e)"), r2(T_RANK), 1.5, None, ALU.is_lt).then_inc(sel_ready, 1)
            link(dve.tensor_scalar(r2(T_SEL), r2(T_RANK), 1.5, None, ALU.is_lt))
            link(dve.tensor_scalar(r2(T_TMP), r2(T_RANK), 0.5, None, ALU.is_lt))
            dve.wait_ge(cnt_done, 1)
            link(dve.tensor_scalar(r(T_POS, TT * NE), ps[:, 1, 0:TT * NE], 1.0, None, ALU.add))
            dve.tensor_scalar(r(T_OVER, NE), ps[:, 1, TT * NE:TT * NE + NE], P + 0.5, None, ALU.is_gt)
            link(dve.tensor_tensor(r2(T_POS), r2(T_POS), r2(T_SEL), ALU.mult))
            for t in range(TT):
                ins = dve.tensor_scalar(r(T_JP + t * JCOLS, NE), r(T_POS + t * NE, NE), -1.0, None, ALU.add)
            link(ins)
            def job_gates(jn):
                for t in range(TT):
                    jg = rt[:, bass.ds(jn + (T_JG + t * JCOLS), 1)]
                    ins = dve.tensor_copy(rt[:, T_GTOK + t:T_GTOK + t + 1], jg)
                return ins

            def choose(jn):
                for t in range(TT):
                    jp = rt[:, bass.ds(jn + (T_JP + t * JCOLS), 1)]
                    ins = dve.tensor_scalar(pick[:, t, :], cst[:, C_IOTA:C_IOTA + P], jp, None, ALU.is_equal)
                ins.then_inc(pick_ready, 1)

            def gathered(j1, halves=(0, 1)):
                for k in range(KD // 2 * halves[0], KD // 2 * (halves[-1] + 1)):
                    if k % 4 == 0:
                        dve.wait_ge(xg_hi_ready, 2 * j1 + (k // 4 + 1))
                    g = gain_rows[3] + k
                    ins = dve.scalar_tensor_tensor(
                        out=xg_lo[:, k, :], in0=ps[:, 1 if k < 4 else 3, (k % 4) * P:(k % 4 + 1) * P],
                        scalar=colpar[:, g:g + 1], in1=xg_hi[:, k, :].bitcast(F32), op0=ALU.mult, op1=ALU.subtract)
                    if k % 4 == 3:
                        ins.then_inc(xg_lo_ready, 1)

            def turned_h(j, i):
                dve.wait_ge(hT_hi, SLABS * j + (i + 1))
                dve.tensor_tensor(mh_lo[:, :, :], ps[:, 4, :].rearrange("p (c f) -> p c f", c=4),
                                  mh_hi[:, :, :].bitcast(F32), ALU.subtract).then_inc(hT_lo, 1)

            def y_out(j):
                for half in range(2):
                    cs = slice(half * 512, half * 512 + 512)
                    dve.wait_ge(y_act, 2 * j + (half + 1))
                    ins = dve.scalar_tensor_tensor(out=y_lo[:, cs], in0=bank(6 + half), scalar=rt[:, T_GSLOT:T_GSLOT + 1],
                                                   in1=y_hi[:, cs].bitcast(F32), op0=ALU.mult, op1=ALU.subtract)
                    ins.then_inc(y_dve, 1)

            def add_out(j):
                dve.wait_ge(comb_done, j + 1)
                dve.wait_ge(lo_ready, j * JOB_UNITS + U_MOE)
                for n, b in enumerate((5, 4, 3, 1)):
                    t, half = divmod(n, 2)
                    v = xres[:, t, half * 512:(half + 1) * 512]
                    ins = dve.tensor_tensor(v, v, bank(b), ALU.add)
                ins.then_inc(comb_added, 1)

            choose(0)
            moe_split_lo(dve, 0, 0)
            dve.wait_ge(exp_ready, 1)
            link(dve.tensor_scalar(r(T_DEN, TT), r(T_EXP, TT), 1.0, None, ALU.add))
            link(dve.reciprocal(r(T_G1, TT), r(T_DEN, TT)))
            link(dve.tensor_tensor(r(T_G2, TT), r(T_G1, TT), r(T_EXP, TT), ALU.mult))
            link(dve.tensor_tensor(r2(T_Q), r2(T_SEL), r2(T_TMP), ALU.subtract))
            for t in range(TT):
                ins = dve.tensor_scalar(r(T_Q + t * NE, NE), r(T_Q + t * NE, NE), r(T_G2 + t), None, ALU.mult)
            link(ins)
            for t in range(TT):
                ins = dve.scalar_tensor_tensor(out=r(T_GATE + t * NE, NE), in0=r(T_TMP + t * NE, NE), scalar=r(T_G1 + t),
                                               in1=r(T_Q + t * NE, NE), op0=ALU.mult, op1=ALU.add)
            link(ins)
            for t in range(TT):
                ins = dve.tensor_copy(r(T_JG + t * JCOLS, NE), r(T_GATE + t * NE, NE))
            link(ins)
            job_gates(0)
            c1 = r(T_CMP, 64).rearrange("p (e f) -> p e f", e=NE)
            link(dve.tensor_tensor(c1, r(T_OVER, NE).unsqueeze(1).broadcast_to([P, NE, NE]),
                                   cst[:, C_LT:C_LT + 64].rearrange("p (e f) -> p e f", e=NE), ALU.mult))
            link(dve.tensor_reduce(r(T_OIDX, NE), c1, AX.X, ALU.add))
            link(dve.scalar_tensor_tensor(out=r2(T_Q), in0=r2(T_SEL), scalar=-float(P), in1=r2(T_POS), op0=ALU.mult, op1=ALU.add))
            for k in range(JOBS_MAX - NE):
                ins = dve.scalar_tensor_tensor(out=r(T_W + k * NE, NE), in0=r(T_OIDX, NE), scalar=float(k), in1=r(T_OVER, NE),
                                               op0=ALU.is_equal, op1=ALU.mult)
            link(ins)
            products = [0]

            def dot(a, b, start, dst):
                at_ = T_CMP2 + products[0] * NE
                products[0] += 1
                return dve.tensor_tensor_reduce(r(at_, NE), a, b, 1.0, start, ALU.mult, ALU.add, dst)

            for k in range(JOBS_MAX - NE):
                w = r(T_W + k * NE, NE)
                for t in range(TT):
                    c = t * JCOLS + NE + k
                    dot(r(T_Q + t * NE, NE), w, -1.0, r(T_JP + c))
                    dot(r(T_GATE + t * NE, NE), w, 0.0, r(T_JG + c))
                ins = dot(cst[:, C_IOTA:C_IOTA + NE], w, 0.0, r(T_F + 2 + k))
            link(ins)
            link(dve.tensor_reduce(r(T_F), r(T_OVER, NE), AX.X, ALU.add))
            link(dve.tensor_scalar(r(T_F), r(T_F), float(NE), None, ALU.add))
            link(dve.memset(r(T_F + 1), float(NE - 1)))
            dve.tensor_copy(meta[:, 0:5], r(T_F, 5)).then_inc(meta_ready, 1)
            gathered(0, (0,))
            for w in range(1, SPLITS - 1):
                moe_split_lo(dve, 0, w)
            gathered(0, (1,))
            dve.wait_ge(y_zeroed, 1)
            dve.wait_ge(meta_ready, 1)
            jobs = dve.value_load(meta[0:1, 0:1], min_val=NE, max_val=JOBS_MAX)
            with dve.Fori(0, jobs) as j:
                y_out(j)
                moe_split_lo(dve, j, SPLITS - 1)
                for v, (kind, i) in enumerate(job_steps):
                    for w in range(4 * v + SPLITS, min(4 * v + 4 + SPLITS, JOB_UNITS + SPLITS - 1)):
                        moe_split_lo(dve, j, w)
                    if kind == "g" and i == 0:
                        add_out(j)
                    if kind == "g" and i >= 1:
                        turned_h(j, i - 1)
                    if kind == "g" and i == 2:
                        dve.wait_ge(pickT_done, j + 1)
                        dve.wait_ge(gather_done, 2 * j + 2)
                        job_gates(j + 1)
                        choose(j + 1)
                    if kind == "u":
                        dve.wait_ge(silu_ready, SLABS * j + (i + 1))
                        dve.wait_ge(unit_used, j * JOB_UNITS + (U_MOE + 4 * v + 4))
                        if i >= 2:
                            dve.wait_ge(hT_done, SLABS * j + (i - 1))
                        dve.tensor_tensor(mh[:, i % 2, :], msg[:, i % 2, :], bank(2 + i % 2), ALU.mult).then_inc(h_ready, 1)
                    if kind == "d" and i == SLABS - 2:
                        turned_h(j, SLABS - 1)
                        gathered(j + 1)
            y_out(jobs)
            for n in range(2 * TT):
                half, t = divmod(n, TT)
                dve.wait_ge(last_done, n + 1)
                v = xres[:, t, half * 512:(half + 1) * 512]
                dve.tensor_tensor(v, v, bank(QUARTER_BANKS[n]), ALU.add).then_inc(last_added, 1)


_INS = ["x", "norm_mix", "norm_ffn", "w_in_ab", "gmlp_v_gain", "gmlp_ws", "gmlp_bs", "dil_q_gain", "dil_k_gain",
        "w_out_ab", "ffn_w_gate", "ffn_w_up", "ffn_w_down", "w_in_cd", "moba_q_gain", "moba_k_gain", "conv_w",
        "w_out_cd", "router_w", "moe_w_gate", "moe_w_up", "moe_w_down"]


def kernel(**inputs):
    import concourse.bacc as bacc
    from concourse.bass_utils import run_bass_kernel_spmd

    nc = bacc.Bacc("TRN2", target_bir_lowering=False, num_devices=1)
    arrays, args = {}, []
    for name in _INS:
        a = np.ascontiguousarray(inputs[name])
        arrays[f"in_{name}"] = a
        args.append(nc.dram_tensor(f"in_{name}", a.shape, mybir.dt.from_np(a.dtype), kind="ExternalInput").ap())
    for name, a in zip(("const_f32", "const_mask"), constant_tables()):
        arrays[name] = a
        args.append(nc.dram_tensor(name, a.shape, mybir.dt.from_np(a.dtype), kind="ExternalInput").ap())
    args.append(nc.dram_tensor("out", (1, SEQ, D), F32, kind="ExternalOutput").ap())
    decoder_trunk(nc, *args)
    r = run_bass_kernel_spmd(nc, [arrays], core_ids=[0])
    return r.results[0]["out"]
```
